# Optimizing a Trainium2 kernel written in Bass

```python
import math
import jax, jax.numpy as jnp
from jax import lax
import numpy as np

D_MODEL = 1024
BATCH = 1
SEQ = 1024
DEPTH = 1
DEC_BATCH = 8
DEC_SEQ = 8
PAST_LEN = 512
PAGE_SIZE = 128

D_MIX = D_MODEL
D_SSM = D_MIX // 2
D_ATTN = D_MIX - D_SSM
SSM_GROUP = 16
N_SSM_GROUPS = D_SSM // SSM_GROUP
SSM_STATE = 64
DT_MIN = 1e-3
DT_MAX = 1e-1
HEAD_DIM = 64
N_HEADS = D_ATTN // HEAD_DIM
D_IN = D_SSM + 3 * D_ATTN + N_HEADS
Q_BLOCK = 128
N_EXPERTS = 64
TOP_K = 6
N_EXPERT_GROUPS = 8
TOPK_GROUPS = 4
D_EXPERT = 256
D_SHARED = 256
ROUTED_SCALE = 2.5
MOE_BLOCK = 128
EPS = 1e-6

kernel_name = 'hymba_s5_fox_moe_adaln_step'

def _rmsnorm(x, g):
    xf = x.astype(jnp.float32)
    xf = xf * lax.rsqrt(jnp.mean(xf * xf, axis=-1, keepdims=True) + EPS)
    return xf * g.astype(jnp.float32)

def _norm_modulate(x, g, shift, scale):
    h = _rmsnorm(x, g) * (1.0 + scale[:, None, :]) + shift[:, None, :]
    return h.astype(x.dtype)

def _adaln(c, w, b, n):
    mod = jax.nn.silu(c.astype(jnp.float32)) @ w.astype(jnp.float32) + b.astype(jnp.float32)
    return jnp.split(mod, n, axis=-1)

def _swiglu(x, wg, wu, wd):
    return (jax.nn.silu(x @ wg) * (x @ wu)) @ wd

def _cmul(ar, ai, br, bi):
    return ar * br - ai * bi, ar * bi + ai * br

def _scan_combine(e1, e2):
    a1r, a1i, b1r, b1i = e1
    a2r, a2i, b2r, b2i = e2
    ar, ai = _cmul(a2r, a2i, a1r, a1i)
    br, bi = _cmul(a2r, a2i, b1r, b1i)
    return ar, ai, br + b2r, bi + b2i

def _s5_scan(u, h0, lam_re, lam_im, log_step, b_re, b_im, c_re, c_im, d_skip):
    f32 = jnp.float32
    lam_re = lam_re.astype(f32)
    lam_im = lam_im.astype(f32)
    dt = jnp.exp(log_step.astype(f32))[:, None]
    mag = jnp.exp(lam_re * dt)
    a_re = mag * jnp.cos(lam_im * dt)
    a_im = mag * jnp.sin(lam_im * dt)
    den = lam_re * lam_re + lam_im * lam_im
    n_re = a_re - 1.0
    f_re = (n_re * lam_re + a_im * lam_im) / den
    f_im = (a_im * lam_re - n_re * lam_im) / den
    b_re = b_re.astype(f32)
    b_im = b_im.astype(f32)
    bb_re = f_re[..., None] * b_re - f_im[..., None] * b_im
    bb_im = f_re[..., None] * b_im + f_im[..., None] * b_re
    bu_re = jnp.einsum('blgi,gpi->blgp', u, bb_re)
    bu_im = jnp.einsum('blgi,gpi->blgp', u, bb_im)
    if h0 is not None:
        init_re, init_im = _cmul(a_re, a_im, h0[0].astype(f32), h0[1].astype(f32))
        bu_re = bu_re.at[:, 0].add(init_re)
        bu_im = bu_im.at[:, 0].add(init_im)
    A_re = jnp.broadcast_to(a_re, bu_re.shape)
    A_im = jnp.broadcast_to(a_im, bu_im.shape)
    _, _, h_re, h_im = lax.associative_scan(_scan_combine, (A_re, A_im, bu_re, bu_im), axis=1)
    y = (jnp.einsum('blgp,gip->blgi', h_re, c_re.astype(f32))
         - jnp.einsum('blgp,gip->blgi', h_im, c_im.astype(f32))
         + d_skip.astype(f32) * u)
    return y, h_re[:, -1], h_im[:, -1]

def _fox_block(q, cq, q_pos, k, v, ck, k_pos):
    s = jnp.einsum('bqhd,bkhd->bhqk', q, k).astype(jnp.float32) * (HEAD_DIM ** -0.5)
    s = s + jnp.transpose(cq, (0, 2, 1))[..., :, None] - jnp.transpose(ck, (0, 2, 1))[..., None, :]
    causal = k_pos[None, :] <= q_pos[:, None]
    s = jnp.where(causal, s, -jnp.inf)
    p = jax.nn.softmax(s, axis=-1)
    return jnp.einsum('bhqk,bkhd->bqhd', p.astype(v.dtype), v)

def _hybrid_mixer(h, past, w_in, b_fgate, lam_re, lam_im, log_step, b_re, b_im, c_re, c_im,
                  d_skip, w_glu, b_glu, g_ssm_out, g_attn_out, w_out):
    Bn, L, _ = h.shape
    f32 = jnp.float32
    proj = h @ w_in
    u = proj[..., :D_SSM]
    q = proj[..., D_SSM:D_SSM + D_ATTN].reshape(Bn, L, N_HEADS, HEAD_DIM)
    k = proj[..., D_SSM + D_ATTN:D_SSM + 2 * D_ATTN].reshape(Bn, L, N_HEADS, HEAD_DIM)
    v = proj[..., D_SSM + 2 * D_ATTN:D_SSM + 3 * D_ATTN].reshape(Bn, L, N_HEADS, HEAD_DIM)
    fg = proj[..., D_SSM + 3 * D_ATTN:]
    logf = jax.nn.log_sigmoid(fg.astype(f32) + b_fgate.astype(f32))

    ug = u.astype(f32).reshape(Bn, L, N_SSM_GROUPS, SSM_GROUP)
    h0 = None if past is None else (past[0], past[1])
    y_ssm, hr, hi = _s5_scan(ug, h0, lam_re, lam_im, log_step, b_re, b_im, c_re, c_im, d_skip)
    y_ssm = jax.nn.gelu(y_ssm.reshape(Bn, L, D_SSM))
    y_ssm = y_ssm * jax.nn.sigmoid(y_ssm @ w_glu.astype(f32) + b_glu.astype(f32))

    if past is None:
        c_all = jnp.cumsum(logf, axis=1)
        nb = L // Q_BLOCK
        k_pos = jnp.arange(L, dtype=jnp.int32)
        qb = q.reshape(Bn, nb, Q_BLOCK, N_HEADS, HEAD_DIM).swapaxes(0, 1)
        cqb = c_all.reshape(Bn, nb, Q_BLOCK, N_HEADS).swapaxes(0, 1)
        pb = k_pos.reshape(nb, Q_BLOCK)
        o = lax.map(lambda a: _fox_block(a[0], a[1], a[2], k, v, c_all, k_pos), (qb, cqb, pb))
        o = o.swapaxes(0, 1).reshape(Bn, L, D_ATTN)
    else:
        k_past, v_past, logf_past = past[2], past[3], past[4]
        n_past = k_past.shape[1]
        k_all = jnp.concatenate([k_past.astype(k.dtype), k], axis=1)
        v_all = jnp.concatenate([v_past.astype(v.dtype), v], axis=1)
        c_all = jnp.cumsum(jnp.concatenate([logf_past.astype(f32), logf], axis=1), axis=1)
        k_pos = jnp.arange(n_past + L, dtype=jnp.int32)
        o = _fox_block(q, c_all[:, n_past:], k_pos[n_past:], k_all, v_all, c_all, k_pos)
        o = o.reshape(Bn, L, D_ATTN)

    merged = jnp.concatenate([_rmsnorm(y_ssm, g_ssm_out), _rmsnorm(o, g_attn_out)], axis=-1)
    out = merged.astype(h.dtype) @ w_out
    return out, (k, v, logf, hr, hi)

def _grouped_experts(x2, idx, wts, w_eg, w_eu, w_ed):
    T, Dm = x2.shape
    K = idx.shape[1]
    E = w_eg.shape[0]
    M = MOE_BLOCK
    A = T * K
    e_flat = idx.reshape(-1).astype(jnp.int32)
    tok_flat = jnp.arange(A, dtype=jnp.int32) // K
    order = jnp.argsort(e_flat, stable=True)
    e_sorted = e_flat[order]
    counts = jnp.bincount(e_flat, length=E).astype(jnp.int32)
    padded = ((counts + M - 1) // M) * M
    pad_end = jnp.cumsum(padded)
    pad_start = pad_end - padded
    start = jnp.cumsum(counts) - counts
    rank = jnp.arange(A, dtype=jnp.int32) - start[e_sorted]
    dest_sorted = pad_start[e_sorted] + rank
    n_rows = (-(-A // M)) * M + E * M
    n_blocks = n_rows // M
    src_tok = jnp.full((n_rows,), T, jnp.int32).at[dest_sorted].set(tok_flat[order])
    x_pad = jnp.concatenate([x2, jnp.zeros((1, Dm), x2.dtype)], axis=0)
    block_start = jnp.arange(n_blocks, dtype=jnp.int32) * M
    block_e = jnp.minimum(jnp.searchsorted(pad_end, block_start, side='right'), E - 1)
    xb = x_pad[src_tok].reshape(n_blocks, M, Dm)

    def run(a):
        xblk, e = a
        return _swiglu(xblk, w_eg[e], w_eu[e], w_ed[e])

    yb = lax.map(run, (xb, block_e)).reshape(n_rows, Dm)
    dest_flat = jnp.zeros((A,), jnp.int32).at[order].set(dest_sorted)
    y = (yb[dest_flat].reshape(T, K, Dm).astype(jnp.float32) * wts[..., None]).sum(axis=1)
    return y.astype(x2.dtype)

def _moe_ffn(h, w_router, router_bias, w_eg, w_eu, w_ed, w_sg, w_su, w_sd):
    Bn, L, Dm = h.shape
    x2 = h.reshape(-1, Dm)
    T = x2.shape[0]
    scores = jax.nn.sigmoid((x2 @ w_router).astype(jnp.float32))
    biased = scores + router_bias.astype(jnp.float32)
    per_group = N_EXPERTS // N_EXPERT_GROUPS
    grp_score = lax.top_k(biased.reshape(T, N_EXPERT_GROUPS, per_group), 2)[0].sum(-1)
    _, top_grp = lax.top_k(grp_score, TOPK_GROUPS)
    grp_mask = jax.nn.one_hot(top_grp, N_EXPERT_GROUPS, dtype=jnp.float32).sum(1) > 0
    expert_mask = jnp.repeat(grp_mask, per_group, axis=1)
    _, idx = lax.top_k(jnp.where(expert_mask, biased, -jnp.inf), TOP_K)
    w = jnp.take_along_axis(scores, idx, axis=1)
    w = w / jnp.sum(w, axis=-1, keepdims=True) * ROUTED_SCALE
    routed = _grouped_experts(x2, idx, w, w_eg, w_eu, w_ed)
    shared = _swiglu(x2, w_sg, w_su, w_sd)
    return (routed + shared).reshape(Bn, L, Dm)

def _block(x, c, past, w_ada, b_ada, g_norm1, w_in, b_fgate, lam_re, lam_im, log_step,
           b_re, b_im, c_re, c_im, d_skip, w_glu, b_glu, g_ssm_out, g_attn_out, w_out,
           g_norm2, w_router, router_bias, w_eg, w_eu, w_ed, w_sg, w_su, w_sd):
    sh1, sc1, gt1, sh2, sc2, gt2 = _adaln(c, w_ada, b_ada, 6)
    h = _norm_modulate(x, g_norm1, sh1, sc1)
    mix, state = _hybrid_mixer(h, past, w_in, b_fgate, lam_re, lam_im, log_step, b_re, b_im,
                               c_re, c_im, d_skip, w_glu, b_glu, g_ssm_out, g_attn_out, w_out)
    x = x + (gt1[:, None, :] * mix.astype(jnp.float32)).astype(x.dtype)
    h = _norm_modulate(x, g_norm2, sh2, sc2)
    ff = _moe_ffn(h, w_router, router_bias, w_eg, w_eu, w_ed, w_sg, w_su, w_sd)
    x = x + (gt2[:, None, :] * ff.astype(jnp.float32)).astype(x.dtype)
    return x, state

def setup_inputs(seed: int = 0) -> dict:
    key = jax.random.key(seed)
    keys = iter(jax.random.split(key, 48))
    f32 = jnp.float32
    D = D_MODEL

    def normal(shape, scale=1.0):
        return scale * jax.random.normal(next(keys), shape, f32)

    def gain(shape):
        return 1.0 + normal(shape, 0.05)

    n_pages = PAST_LEN // PAGE_SIZE
    n_used = DEC_BATCH * n_pages
    n_phys = n_used + n_used // 4
    page_table = jax.random.permutation(next(keys), n_phys)[:n_used].reshape(DEC_BATCH, n_pages).astype(jnp.int32)

    x_prompt = normal((BATCH, SEQ, D))
    x_sample = normal((DEC_BATCH, DEC_SEQ, D))
    c_prompt = normal((BATCH, D))
    c_sample = normal((DEC_BATCH, D))
    cache_k = normal((DEPTH, n_phys, PAGE_SIZE, N_HEADS, HEAD_DIM))
    cache_v = normal((DEPTH, n_phys, PAGE_SIZE, N_HEADS, HEAD_DIM))
    cache_logf = jax.nn.log_sigmoid(4.5 + normal((DEPTH, n_phys, PAGE_SIZE, N_HEADS)))
    state_ssm_re = normal((DEPTH, DEC_BATCH, N_SSM_GROUPS, SSM_STATE), 0.3)
    state_ssm_im = normal((DEPTH, DEC_BATCH, N_SSM_GROUPS, SSM_STATE), 0.3)

    w_ada = normal((DEPTH, D, 6 * D), 0.5 * D ** -0.5)
    b_ada = normal((DEPTH, 6 * D), 0.02)
    g_norm1 = gain((DEPTH, D))
    w_in = jnp.concatenate([normal((DEPTH, D, D_SSM + 3 * D_ATTN), D ** -0.5),
                            normal((DEPTH, D, N_HEADS), 0.3 * D ** -0.5)], axis=-1)
    b_fgate = jax.random.uniform(next(keys), (DEPTH, N_HEADS), f32, 3.0, 6.0)
    ssm_lambda_re = -0.5 + normal((DEPTH, N_SSM_GROUPS, SSM_STATE), 0.01)
    ssm_lambda_im = math.pi * jnp.arange(SSM_STATE, dtype=f32)[None, None, :] + normal((DEPTH, N_SSM_GROUPS, SSM_STATE), 0.01)
    ssm_log_step = jax.random.uniform(next(keys), (DEPTH, N_SSM_GROUPS), f32, math.log(DT_MIN), math.log(DT_MAX))
    ssm_b_re = normal((DEPTH, N_SSM_GROUPS, SSM_STATE, SSM_GROUP), (2 * SSM_GROUP) ** -0.5)
    ssm_b_im = normal((DEPTH, N_SSM_GROUPS, SSM_STATE, SSM_GROUP), (2 * SSM_GROUP) ** -0.5)
    ssm_c_re = normal((DEPTH, N_SSM_GROUPS, SSM_GROUP, SSM_STATE), (2 * SSM_STATE) ** -0.5)
    ssm_c_im = normal((DEPTH, N_SSM_GROUPS, SSM_GROUP, SSM_STATE), (2 * SSM_STATE) ** -0.5)
    ssm_d = normal((DEPTH, N_SSM_GROUPS, SSM_GROUP))
    w_glu = normal((DEPTH, D_SSM, D_SSM), D_SSM ** -0.5)
    b_glu = normal((DEPTH, D_SSM), 0.02)
    g_ssm_out = gain((DEPTH, D_SSM))
    g_attn_out = gain((DEPTH, D_ATTN))
    w_out = normal((DEPTH, D_MIX, D), D_MIX ** -0.5)
    g_norm2 = gain((DEPTH, D))
    w_router = normal((DEPTH, D, N_EXPERTS), D ** -0.5)
    router_bias = normal((DEPTH, N_EXPERTS), 0.01)
    w_exp_gate = normal((DEPTH, N_EXPERTS, D, D_EXPERT), D ** -0.5)
    w_exp_up = normal((DEPTH, N_EXPERTS, D, D_EXPERT), D ** -0.5)
    w_exp_down = normal((DEPTH, N_EXPERTS, D_EXPERT, D), D_EXPERT ** -0.5)
    w_sh_gate = normal((DEPTH, D, D_SHARED), D ** -0.5)
    w_sh_up = normal((DEPTH, D, D_SHARED), D ** -0.5)
    w_sh_down = normal((DEPTH, D_SHARED, D), D_SHARED ** -0.5)
    g_final = gain((D,))
    w_ada_final = normal((D, 2 * D), 0.5 * D ** -0.5)
    b_ada_final = normal((2 * D,), 0.02)
    return {'x_prompt': x_prompt, 'x_sample': x_sample, 'c_prompt': c_prompt, 'c_sample': c_sample,
            'cache_k': cache_k, 'cache_v': cache_v, 'cache_logf': cache_logf,
            'state_ssm_re': state_ssm_re, 'state_ssm_im': state_ssm_im, 'page_table': page_table,
            'w_ada': w_ada, 'b_ada': b_ada, 'g_norm1': g_norm1, 'w_in': w_in, 'b_fgate': b_fgate,
            'ssm_lambda_re': ssm_lambda_re, 'ssm_lambda_im': ssm_lambda_im, 'ssm_log_step': ssm_log_step,
            'ssm_b_re': ssm_b_re, 'ssm_b_im': ssm_b_im, 'ssm_c_re': ssm_c_re, 'ssm_c_im': ssm_c_im,
            'ssm_d': ssm_d, 'w_glu': w_glu, 'b_glu': b_glu, 'g_ssm_out': g_ssm_out,
            'g_attn_out': g_attn_out, 'w_out': w_out, 'g_norm2': g_norm2, 'w_router': w_router,
            'router_bias': router_bias, 'w_exp_gate': w_exp_gate, 'w_exp_up': w_exp_up,
            'w_exp_down': w_exp_down, 'w_sh_gate': w_sh_gate, 'w_sh_up': w_sh_up,
            'w_sh_down': w_sh_down, 'g_final': g_final, 'w_ada_final': w_ada_final,
            'b_ada_final': b_ada_final}

def reference(x_prompt, x_sample, c_prompt, c_sample, cache_k, cache_v, cache_logf,
              state_ssm_re, state_ssm_im, page_table, w_ada, b_ada, g_norm1, w_in, b_fgate,
              ssm_lambda_re, ssm_lambda_im, ssm_log_step, ssm_b_re, ssm_b_im, ssm_c_re, ssm_c_im,
              ssm_d, w_glu, b_glu, g_ssm_out, g_attn_out, w_out, g_norm2, w_router, router_bias,
              w_exp_gate, w_exp_up, w_exp_down, w_sh_gate, w_sh_up, w_sh_down, g_final,
              w_ada_final, b_ada_final):
    n_seq, n_pages = page_table.shape
    n_past = n_pages * PAGE_SIZE
    xp, xs = x_prompt, x_sample
    kp, vp, lfp, srp, sip = [], [], [], [], []
    ks, vs, lfs, srs, sis = [], [], [], [], []
    for l in range(DEPTH):
        lp = dict(w_ada=w_ada[l], b_ada=b_ada[l], g_norm1=g_norm1[l], w_in=w_in[l],
                  b_fgate=b_fgate[l], lam_re=ssm_lambda_re[l], lam_im=ssm_lambda_im[l],
                  log_step=ssm_log_step[l], b_re=ssm_b_re[l], b_im=ssm_b_im[l],
                  c_re=ssm_c_re[l], c_im=ssm_c_im[l], d_skip=ssm_d[l], w_glu=w_glu[l],
                  b_glu=b_glu[l], g_ssm_out=g_ssm_out[l], g_attn_out=g_attn_out[l],
                  w_out=w_out[l], g_norm2=g_norm2[l], w_router=w_router[l],
                  router_bias=router_bias[l], w_eg=w_exp_gate[l], w_eu=w_exp_up[l],
                  w_ed=w_exp_down[l], w_sg=w_sh_gate[l], w_su=w_sh_up[l], w_sd=w_sh_down[l])
        k_past = cache_k[l][page_table].reshape(n_seq, n_past, N_HEADS, HEAD_DIM)
        v_past = cache_v[l][page_table].reshape(n_seq, n_past, N_HEADS, HEAD_DIM)
        logf_past = cache_logf[l][page_table].reshape(n_seq, n_past, N_HEADS)
        past = (state_ssm_re[l], state_ssm_im[l], k_past, v_past, logf_past)
        xp, st_p = _block(xp, c_prompt, None, **lp)
        xs, st_s = _block(xs, c_sample, past, **lp)
        kp.append(st_p[0]); vp.append(st_p[1]); lfp.append(st_p[2]); srp.append(st_p[3]); sip.append(st_p[4])
        ks.append(st_s[0]); vs.append(st_s[1]); lfs.append(st_s[2]); srs.append(st_s[3]); sis.append(st_s[4])
    shp, scp = _adaln(c_prompt, w_ada_final, b_ada_final, 2)
    shs, scs = _adaln(c_sample, w_ada_final, b_ada_final, 2)
    y_prompt = _norm_modulate(xp, g_final, shp, scp)
    y_sample = _norm_modulate(xs, g_final, shs, scs)
    return (y_prompt, y_sample, jnp.stack(kp), jnp.stack(vp), jnp.stack(lfp), jnp.stack(srp), jnp.stack(sip),
            jnp.stack(ks), jnp.stack(vs), jnp.stack(lfs), jnp.stack(srs), jnp.stack(sis))


_drawn_inputs = setup_inputs


def setup_inputs(seed=0):
    import zlib

    import numpy as np

    out = dict(_drawn_inputs(seed))
    spreads = {}
    factors = {'ssm_lambda_re': 3.723, 'b_glu': 6.293}
    for name, (base, spread) in spreads.items():
        noise = np.random.default_rng([zlib.crc32(name.encode()), seed]).standard_normal(out[name].shape)
        drawn = base * np.exp(spread * noise) if base else spread * noise
        out[name] = __import__('jax').numpy.asarray(drawn.astype(out[name].dtype))
    for name, factor in factors.items():
        out[name] = (out[name] * factor).astype(out[name].dtype)
    return out
```

```python
from contextlib import ExitStack

import numpy as np
import concourse.bass as bass
from concourse import mybir

ALU = mybir.AluOpType
ACT = mybir.ActivationFunctionType
F32 = mybir.dt.float32
BF16 = mybir.dt.bfloat16
I32 = mybir.dt.int32
AX = mybir.AxisListType

P = 128
D = 1024
KD = D // P
SEQ = 1024
CH = 8
NC_ = SEQ // CH
NSEQ = 8
NS = NSEQ * CH
T = SEQ + NS
NT = 9
H = 8
DH = 64
DA = H * DH
KA = DA // P
G = 32
GP = G // 2
GI = 16
NST = 64
PAGES = 4
PAGE = 128
PAST = PAGES * PAGE
E = 64
TOPK = 6
TOPG = 4
FE = 256
SCALE_ROUTED = 2.5
EPS = 1e-6
NM = 9
NADA = 12
NADF = 4
NEG = -1e30
MAGIC = 12582912.0
MAXPAIR = (T * TOPK // P + E + 1) // 2
RING = 4
MAXBLK = 128
TWO_PI = 2.0 * np.pi
C1 = 6.28125
C2 = TWO_PI - C1
PI_SAFE = 3.1415925
IN_COLS = DA + 3 * DA + H


def rows(t):
    return P if t < 8 else NS


class Slots:

    def __init__(self, filled, drained):
        self.filled, self.drained = filled, drained
        self.count = [0] * len(filled)
        self.use = {}

    def fill(self, pe, key, s):
        if self.count[s]:
            pe.wait_ge(self.drained[s], self.count[s])
        self.count[s] += 1
        self.use[key] = (s, self.count[s])

    def full(self, ins, key):
        ins.then_inc(self.filled[self.use[key][0]], 1)

    def wait_full(self, eng, key):
        s, n = self.use[key]
        eng.wait_ge(self.filled[s], n)

    def empty(self, ins, key):
        ins.then_inc(self.drained[self.use[key][0]], 1)

    def wait_empty(self, eng, key):
        s, n = self.use[key]
        eng.wait_ge(self.drained[s], n)


def hymba_program(nc, ap, out):
    ctx = ExitStack()
    with ctx:
        def sem(name):
            return ctx.enter_context(nc.semaphore(name))

        arena_t = ctx.enter_context(nc.sbuf_tensor("arena", [P, 48928], F32))
        tail_t = ctx.enter_context(nc.sbuf_tensor("tail", [P, 4280], F32))
        psum = ctx.enter_context(nc.psum_tensor("psum", [P, 8, 512], F32))
        h2_dram = nc.dram_tensor("h2_rows", (T, D), F32, kind="Internal").ap()
        y_dram = nc.dram_tensor("moe_rows", (T + P, D), F32, kind="Internal").ap()

        def arena(at, *shape, dt=F32, parts=P):
            n = int(np.prod(shape))
            v = arena_t[0:parts, at:at + (n if dt != BF16 else (n + 1) // 2)]
            if dt != F32:
                v = v.bitcast(dt)
            names = "abcd"[:len(shape)]
            if len(shape) > 1:
                v = v.rearrange(f"p ({' '.join(names)}) -> p {' '.join(names)}", **dict(zip(names[1:], shape[1:])))
            return v

        tail_at = [0]

        def small(*shape, dt=F32, parts=P):
            n = int(np.prod(shape))
            n4 = n if dt != BF16 else (n + 1) // 2
            at = tail_at[0]
            tail_at[0] += n4
            assert tail_at[0] <= 4280, tail_at
            v = tail_t[0:parts, at:at + n4]
            if dt != F32:
                v = v.bitcast(dt)
            names = "abcd"[:len(shape)]
            if len(shape) > 1:
                v = v.rearrange(f"p ({' '.join(names)}) -> p {' '.join(names)}", **dict(zip(names[1:], shape[1:])))
            return v

        slot = [psum[:, 0:2, :].rearrange("p a b -> p (a b)"), psum[:, 2:4, :].rearrange("p a b -> p (a b)")] + [psum[:, b, :] for b in range(4, 8)]
        slots = Slots([sem(f"slot_filled{i}") for i in range(6)], [sem(f"slot_drained{i}") for i in range(6)])

        ident = small(P)
        iota_row = small(P)
        iota_part = small(1)
        ones_col = small(1)
        pack_t = small(100)
        mod_t = small(64, NM)
        a1 = small(KD, NM)
        a2 = small(KD, NM)
        af = small(KD, NM)
        tri = small(P, dt=BF16)
        ones_b = small(P, dt=BF16)
        rstd = small(NT)
        ssq = small(NT)
        x_buf = small(2, D)
        hT = arena(0, KD, T)
        ada_w = arena(8704, 2, KD, 512)
        U = arena(8704, G, NC_ + NSEQ)
        Hp = arena(13056, 2, GP, NC_ + 1)
        w_u = arena(17184, KD, 512)
        S = arena(17184, 2, GP, NC_ + NSEQ)
        u = arena(21536, G, CH, GI)
        Ksb = arena(21536, G, P, parts=GI)
        pw = arena(21536, 2, GP, 9)
        pwr = arena(21824, 2, GP, 8)
        b_raw = arena(22080, 2, GP, GI)
        c_l1 = arena(22592, 2, GP, GI)
        bb = arena(23104, 2, GP, GI)
        s5_small = arena(23616, 24, GP)
        BP = arena(25632, 2, GP, 8, GI)
        u8 = arena(25632, G, CH, GI, parts=NSEQ)
        CP = arena(29728, 2, GP, 9, GI)
        BS = arena(34336, GP, 2, 2, NST)
        M = arena(38432, G, P)
        mod_row = arena(38432, 2, 512, parts=NM)
        Etab = arena(42528, 2, GP, NC_)
        pack = arena(42528, P, parts=100)
        pack2 = arena(42656, P, parts=48)
        d_raw = arena(42784, GI, parts=G)
        step_raw = arena_t[32:48, 45616:45618]
        h0_raw = arena(42800, 2, P)
        c_raw = arena(43056, 4, P)
        cond = arena(43568, D, parts=NM)
        cond_act = arena(44592, D, parts=NM)
        tmp = arena(46624, 2304)
        u_s = arena(46624, DA, parts=NS)
        y_s = arena(47136, DA, parts=NS)
        prm = small(48)
        h0_t = small(2, NSEQ, GP)
        cs_t = small(KD, NM)
        d_t = small(G, parts=GI)
        mag8 = small(GP)
        fin_p = small(2, GP)
        fin_s = small(2, NSEQ, GP)
        yT = arena(30240, KA, T)
        w_glu = x_buf.rearrange("p a (b n) -> p (a b) n", n=DA)
        ysT = arena(34848, KA, T)
        sq = arena(39200, KA, 512)
        w_q = arena(8704, KD, IN_COLS - DA)
        qT = arena(21536, H, T)
        v = arena(30240, NT, DA)
        kT = arena(41248, KA, T)
        k_tok = arena(45600, 2, DA)
        lf = arena(46624, T, parts=H)
        lf_a = arena(47712, T, parts=H)
        sc = arena(8192, 2, SEQ)
        pr = arena(10240, 2, SEQ)
        pt = arena(12288, 2, SEQ)
        o_tok = arena(14336, NT, DA)
        c_row = arena(18944, T, parts=H)
        neg_c = [arena(20032, SEQ), arena(39200, SEQ)]
        kpg = arena(0, 2, PAGES, DA)
        vpg = arena(4096, 2, PAGES, DA)
        k_ts = arena(8192, 2, KA, PAST)
        q_bd = arena(12288, NSEQ, KA, NS)
        s_s = arena(19456, PAST + CH, parts=NS)
        p_s = arena(19976, PAST + CH, parts=NS)
        p_ts = arena(20496, PAGES + 1, NS)
        v_new = arena(45600, 2, DA, parts=CH)
        head_mask = arena(47712, DA, parts=NS)
        o_masked = arena(48224, DA, parts=NS)
        lf_pages = x_buf.rearrange("p a b -> p (a b)")[:, 0:256].rearrange("p (j n) -> p j n", j=PAGES)
        lf_s = x_buf.rearrange("p a b -> p (a b)")[0:NS, 256:776]
        c_s = x_buf.rearrange("p a b -> p (a b)")[0:NS, 776:1296]
        sel_seq = x_buf.rearrange("p a b -> p (a b)")[0:NS, 1296:1808].rearrange("p (b n) -> p b n", b=NSEQ)
        sel_row = x_buf.rearrange("p a b -> p (a b)")[0:NS, 1808:1928]
        new_mask = x_buf.rearrange("p a b -> p (a b)")[0:NS, 1928:1936]
        same_tok = x_buf.rearrange("p a b -> p (a b)")[0:NS, 1936:1944]
        s_one = x_buf.rearrange("p a b -> p (a b)")[0:NS, 1944:1952]
        causal = small(P)
        att_one = small(16)
        w_out = arena(21536, KD, D)
        oT = arena(0, KA, T)
        h2T = arena(4352, KD, T)
        x1 = arena(39200, NT, D)
        gate_rows = arena(29728, 2, D)
        h2_tok = arena(31776, 2, D)
        w_router = arena(33824, KD, E)
        a8 = small(2, GP)
        b_fg = small(1, parts=H)
        rstd_y = small(NT)
        pages_t = small(NSEQ * PAGES, parts=1).bitcast(I32)
        y = arena(21536, CH, G, GI)
        y8 = arena(25632, CH, G, GI, parts=NSEQ)
        sq_junk = arena(13056, D)
        fin_out = arena(47648, 2, 2 * P)
        sig = arena(45600, 2, 512)
        lf_b = x_buf.rearrange("p a b -> p (a b)")[0:H, 0:T]
        lf_c = arena(39200, T, parts=H)
        lf_tok = arena(40288, NT * H)
        c_tok = arena(40432, CH * H)
        sq_o = arena(8704, DA)
        sq_x1 = arena(4352, D)
        gate_s = arena(9216, KD, NS)
        fin_s_cols = arena(19456, 3, KD, NS)
        h2_row = arena(0, 2, D)
        sh_gu = arena(13056, KD, 2 * FE)
        sh_d = arena(17152, 2, D)
        ring = arena(4096, RING, 12, 512)
        x_rows = arena(0, 2, D)
        xTs = arena(2048, 2, KD, P)
        y_buf = arena(31776, 2, D)
        sh_g = arena(33824, 2, FE)
        sh_u = [arena(19200, FE), arena(4096, FE)]
        e_g = sh_g
        h_row = arena(48416, 2, FE)
        scores = arena(34336, NT, E)
        biased = arena(34912, NT, E)
        masked = arena(35488, NT, E)
        sel_f = arena(36064, NT, E)
        rank = arena(36640, NT, E)
        sort8 = arena(37216, NT, 8, 8)
        sel_b = arena(37792, NT, E, dt=BF16)
        g_score = arena(38080, NT, 8)
        g_left = arena(38152, NT, 8)
        top8 = arena(38224, NT, 8)
        cnt = arena(38296, E)
        nblk = arena(38360, E)
        ends = arena(38424, E)
        below = arena(38488, E)
        r_bias = arena(38552, E)
        blk_expert = arena(38616, 1)
        blk_base = arena(38617, 1)
        blk_tmp = arena(38618, 1)
        pad_row = arena(38619, 1)
        denom = arena(38620, NT)
        n_pairs_t = arena(38629, 1, parts=1).bitcast(I32)
        slot_cols = arena(38716, 2, 5)
        slot_v = arena(38636, 3)
        g_idx = arena(38644, 2).bitcast(I32)
        s_idx = arena(38646, 2).bitcast(I32)
        blk_rank = arena(38648, 2, NT)
        tok_cols = arena(38668, 2, NT, 5, dt=BF16)
        onehot = arena(28672, 2, NT, P, dt=BF16)
        xb = x_buf.rearrange("p a b -> p (a b)")
        tok_all = xb[:, 0:1440].bitcast(BF16).rearrange("p (t e c) -> p t e c", t=NT, e=E)
        base_t = xb[:, 1440:1568]
        expert_i = xb[0:1, 1568:1696].bitcast(I32)
        ring_i = arena(35488, MAXBLK, parts=1).bitcast(I32)
        blk_ord = arena(38727, 1)
        blk_ring = arena(38728, 1)
        ord_expert = arena(38729, 1)
        ord_release = arena(38730, 1)
        filled_experts = arena(35744, E)
        order_i = arena(35616, MAXBLK, parts=1).bitcast(I32)
        ord_i = arena(35808, MAXBLK, parts=1).bitcast(I32)
        release_i = arena(35936, MAXBLK, parts=1).bitcast(I32)
        row_all = arena(36064, MAXBLK)
        w_all = arena(36192, MAXBLK)
        hTs = xb[:, 1696:1952].rearrange("p (k c) -> p k c", k=2)
        y_zero = arena(30720, D)
        fin_rows = arena(21536, 6, D)
        y_rows = arena(4352, NT, D)
        sq_junk2 = y_buf[:, 0, :]
        CHUNKS = [(0, 512), (512, 1024), (1024, T)]
        ATT = [(i, h) for h in range(H) for i in range(8)]
        N_PACK = 45
        N_PHYS = ap["cache_k"].shape[1]

        GLU_TILES = (range(0, 8), range(8, 9), range(0))
        CB_AT = 3

        def pt_keys(it):
            return range(0, ATT[it][0] + 1, 4)

        def groups_of(q):
            return range(8 * (q // 2) + q % 2, 8 * (q // 2 + 1), 2)

        def y_tile(t):
            return y[:, t].rearrange("p g i -> p (g i)")

        def square_y(act, i):
            n, m = divmod(i, KA)
            c0, c1 = CHUNKS[n]
            act.wait_ge(ys_ready, i + 1)
            if n and m == 0:
                slots.wait_full(act, ("SS", n - 1))
            act.activation(sq[:, m, 0:c1 - c0], ysT[:, m, c0:c1], ACT.Square).then_inc(sq_ready, 1)

        ld = {n: sem(f"ld_{n}") for n in ("pack", "step", "cond", "bc", "wu", "wglu", "wq", "wout", "router", "fgate")}
        ld_ada = [sem("ld_ada0"), sem("ld_ada1")]
        ld_x = [sem("ld_x0"), sem("ld_x1")]
        ld_res = sem("ld_res")
        ld_page = [sem("ld_page0"), sem("ld_page1")]
        ld_vpage = [sem("ld_vpage0"), sem("ld_vpage1")]
        y_scaled = sem("y_scaled")
        ld_lfp = sem("ld_lfp")
        ld_pt = sem("ld_pt")
        ld_vnew = [sem("ld_vnew0"), sem("ld_vnew1")]
        stored = sem("stored")
        stored_k = [sem("stored_k0"), sem("stored_k1")]
        moved = sem("moved")
        toeplitz = sem("toeplitz")
        lf_moved = sem("lf_moved")
        n_stored = [0]
        consts = sem("consts")
        m_zero = sem("m_zero")
        q_zero = sem("q_zero")
        dve_step = sem("dve_step")
        act_step = sem("act_step")
        pool_step = sem("pool_step")
        s5_angles = sem("s5_angles")
        s5_trig = sem("s5_trig")
        e_angle = sem("e_angle")
        e_table = sem("e_table")
        s5_mats = sem("s5_mats")
        k_ready = sem("k_ready")
        cs_ready = sem("cs_ready")
        mod_done = sem("mod_done")
        x_sq = sem("x_sq")
        x_var = sem("x_var")
        x_std = sem("x_std")
        xn_ready = sem("xn_ready")
        state_ready = sem("state_ready")
        fin_ready = sem("fin_ready")
        sig_ready = sem("sig_ready")
        ys_ready = sem("ys_ready")
        sq_ready = sem("sq_ready")
        ss_copied = sem("ss_copied")
        fg_ready = sem("fg_ready")
        fg_step = sem("fg_step")
        s_ready = sem("s_ready")
        p_ready = sem("p_ready")
        o_ready = sem("o_ready")
        recip_ready = sem("recip_ready")
        wout_scaled = sem("wout_scaled")
        smp_sel = sem("smp_sel")
        smp_c = sem("smp_c")
        smp_q = sem("smp_q")
        smp_s = sem("smp_s")
        smp_p = sem("smp_p")
        smp_om = sem("smp_om")
        (ones_set, fg_exp, ss_root, smp_pool, gate_ready, rows_stored, o_done, o_sq, x1_ready, x1_sq, xn2_ready, rstd2_ready, h2_ready, scores_ready,
         sh_gu_out, sh_h, ys2_ready, routed, blocks_ready, table_ready, shared_stored, ld_rb, ld_shared, idx_mm, turned, gu_done,
         ht_turned, down_done, onehot_ready, idx_read, xt_copied, h_done, ht_copied, y_act, y_dve, scatter_done, idx_done, g_done,
         rank_step, slot_step, row_step, pool_tick, scattered, routed_done, rows_ready, x2_ready, x2_sq, y_out_ready, pad_scores, cols_ready) = (sem(n) for n in (
            "ones_set fg_exp ss_root smp_pool gate_ready rows_stored o_done o_sq x1_ready x1_sq xn2_ready rstd2_ready h2_ready scores_ready "
            "sh_gu_out sh_h ys2_ready routed blocks_ready table_ready shared_stored ld_rb ld_shared idx_mm turned gu_done "
            "ht_turned down_done onehot_ready idx_read xt_copied h_done ht_copied y_act y_dve scatter_done idx_done g_done "
            "rank_step slot_step row_step pool_tick scattered routed_done rows_ready x2_ready x2_sq y_out_ready pad_scores cols_ready").split())
        ld_ring = [sem(f"ld_ring{i}") for i in range(RING)]
        weights_in = sem("weights_in")
        gathered, stored_h2, stored_ys = ([sem(f"{n}{i}") for i in range(2)] for n in "gathered stored_h2 stored_ys".split())
        ld_y = [sem(f"ld_y{t}") for t in range(NT)]
        steps = {"dve": 0, "act": 0, "pool": 0}

        def dlink(ins):
            steps["dve"] += 1
            ins.then_inc(dve_step, 1)
            nc.vector.wait_ge(dve_step, steps["dve"])

        def alink(ins):
            steps["act"] += 1
            ins.then_inc(act_step, 1)
            nc.scalar.wait_ge(act_step, steps["act"])

        def plink(ins):
            steps["pool"] += 1
            ins.then_inc(pool_step, 1)
            nc.gpsimd.wait_ge(pool_step, steps["pool"])

        def store(eng, dst, src, s=None, n=16):
            if s is None:
                n_stored[0] += 16
                eng.dma_start(dst, src).then_inc(stored, 16)
            else:
                eng.dma_start(dst, src).then_inc(s, 16)

        hT_tile = hT[:, :, 0:SEQ].rearrange("p k (c t) -> p t k c", t=CH)

        def tile_of(buf, t, k=None):
            if t == 8:
                return buf[:, :, SEQ:T] if k is None else buf[:, k, SEQ:T]
            v_ = buf[:, :, 0:SEQ].rearrange("p k (c t) -> p t k c", t=CH)[:, t]
            return v_ if k is None else v_[:, k]

        block = ctx.enter_context(nc.Block())

        @block.tensor
        def _(pe):
            fill, full = slots.fill, slots.full
            pe.wait_ge(consts, 7)
            pe.wait_ge(cs_ready, 1)
            fill(pe, "CS", 5)
            for k in range(KD):
                ins = pe.transpose(slot[5][:, k * NM:(k + 1) * NM], cond_act[:, k * P:(k + 1) * P], ident[0:NM, 0:NM])
            full(ins, "CS")
            slots.wait_empty(pe, "CS")

            def turn_parameters():
                pe.wait_ge(ld["pack"], 16 * N_PACK)
                fill(pe, "T0", 0)
                pe.transpose(slot[0][:, 0:100], pack[:, :], ident[0:100, 0:100])
                pe.transpose(slot[0][:, 128:176], pack2[:, :], ident[0:48, 0:48])
                full(pe.transpose(slot[0][0:GI, 192:192 + G], d_raw[:, :], ident[0:G, 0:G]), "T0")
                fill(pe, "T1", 1)
                pe.transpose(slot[1][:, 0:P], h0_raw[:, 0, :], ident)
                full(pe.transpose(slot[1][:, P:2 * P], h0_raw[:, 1, :], ident), "T1")
                fill(pe, "T2", 4)
                for i in range(4):
                    ins = pe.transpose(slot[4][:, i * P:(i + 1) * P], c_raw[:, i, :], ident)
                full(ins, "T2")

            def turn_mod(n):
                slots.wait_empty(pe, ("ADA", n))
                fill(pe, ("ADT", n), 4 + n % 2)
                for i in range(4):
                    ins = pe.transpose(slot[4 + n % 2][:, i * NM:(i + 1) * NM], mod_row[:, n % 2, i * P:(i + 1) * P], ident[0:NM, 0:NM])
                full(ins, ("ADT", n))

            for n in range(NADA + NADF):
                pe.wait_ge(ld_ada[n % 2], 16 * (n // 2 + 1))
                fill(pe, ("ADA", n), 2 + n % 2)
                for k in range(KD):
                    ins = pe.matmul(slot[2 + n % 2][0:NM, :], cs_t[:, k, :], ada_w[:, n % 2, k, :], start=(k == 0), stop=(k == KD - 1))
                full(ins, ("ADA", n))
                if n == 0:
                    turn_parameters()
                if n:
                    turn_mod(n - 1)
            turn_mod(NADA + NADF - 1)

            pe.wait_ge(s5_mats, 2)
            for q in range(8):
                fill(pe, ("BS", q), 2 + q % 2)
                for i in range(4):
                    gp, ri = 2 * q + i // 2, i % 2
                    ins = pe.transpose(slot[2 + q % 2][:, i * P:(i + 1) * P], BP[:, ri, gp].rearrange("p t j -> p (t j)"), ident)
                full(ins, ("BS", q))
            for q in range(8):
                fill(pe, ("K", q), 4 + q % 2)
                for i, g in enumerate(groups_of(q)):
                    h = NST * (g % 2)
                    for ri in range(2):
                        ins = pe.matmul(slot[4 + q % 2][0:GI, i * P:(i + 1) * P], BP[h:h + NST, ri, g // 2, 7, :],
                                        CP[h:h + NST, ri, g // 2, 0:8, :].rearrange("p n i -> p (n i)"), start=(ri == 0), stop=(ri == 1))
                full(ins, ("K", q))

            def project_u(t):
                slots.wait_empty(pe, ("X", t))
                if t == 0:
                    pe.wait_ge(ld["wu"], 16)
                fill(pe, ("U", t), 2 + t % 2)
                for k in range(KD):
                    ins = pe.matmul(slot[2 + t % 2][0:rows(t), :], tile_of(hT, t, k), w_u[:, k, :], start=(k == 0), stop=(k == KD - 1))
                full(ins, ("U", t))

            for t in range(NT):
                pe.wait_ge(xn_ready, t + 1)
                fill(pe, ("X", t), t % 2)
                for k in range(KD):
                    ins = pe.transpose(slot[t % 2][:, k * P:k * P + rows(t)], x_buf[0:rows(t), t % 2, k * P:(k + 1) * P], ident[0:rows(t), 0:rows(t)])
                full(ins, ("X", t))
                if t:
                    project_u(t - 1)
            project_u(NT - 1)
            slots.wait_empty(pe, ("U", 7))
            for q in range(8):
                fill(pe, ("UT", q), 4 + q % 2)
                for i in range(4):
                    ins = pe.transpose(slot[4 + q % 2][:, i * P:(i + 1) * P], u[:, 4 * q + i].rearrange("p t i -> p (t i)"), ident)
                full(ins, ("UT", q))
            pe.wait_ge(moved, 16 * CH)
            fill(pe, "UTS", 2)
            for g in range(G):
                ins = pe.transpose(slot[2][:, g * NSEQ:(g + 1) * NSEQ], u8[:, g].rearrange("p t i -> p (t i)"), ident[0:NSEQ, 0:NSEQ])
            full(ins, "UTS")
            slots.wait_empty(pe, "UTS")
            slots.wait_empty(pe, ("UT", 7))
            slots.wait_empty(pe, ("UT", 6))
            for gp in range(GP):
                b = (0, 1, 3)[gp % 3]
                fill(pe, ("S", gp), b)
                for g2 in range(2):
                    for ri in range(2):
                        ins = pe.matmul(slot[b][NST * g2:NST * (g2 + 1), ri * 136:(ri + 1) * 136], BS[:, gp, g2, ri, :], U[:, 2 * gp + g2, :], start=True, stop=True)
                full(ins, ("S", gp))
            pe.wait_ge(toeplitz, 16 * CH)
            for q in range(8):
                pe.wait_ge(state_ready, q // 2 + 1)
                for smp in range(2):
                    b = (2 + q % 2) if not smp else (4 + q % 2)
                    m = NSEQ if smp else P
                    fill(pe, ("Y", q, smp), b)
                    for i, g in enumerate(groups_of(q)):
                        h = NST * (g % 2)
                        o = slot[b][0:m, i * P:(i + 1) * P]
                        pe.matmul(o, U[:, g, NC_:] if smp else U[:, g, 0:NC_], M[:, g, :], start=True, stop=False)
                        for ri in range(2):
                            st = h0_t[h:h + NST, ri, :, g // 2] if smp else Hp[h:h + NST, ri, g // 2, 0:NC_]
                            ins = pe.matmul(o, st, CP[h:h + NST, ri, g // 2, 1:9, :].rearrange("p n i -> p (n i)"), start=False, stop=(ri == 1))
                    full(ins, ("Y", q, smp))
            pe.wait_ge(fin_ready, 1)
            fill(pe, "FIN", 0)
            for ri in range(2):
                pe.transpose(slot[0][0:GP, ri * P:(ri + 1) * P], fin_p[:, ri], ident)
                ins = pe.transpose(slot[0][:, 512 + ri * P:512 + (ri + 1) * P], fin_s[:, ri].rearrange("p b g -> p (b g)"), ident)
            full(ins, "FIN")
            slots.wait_empty(pe, ("Y", 7, 0))

            def turn_y(t):
                if t == 8:
                    pe.wait_ge(moved, 32 * CH)
                fill(pe, ("YT", t), 2 + t % 2)
                for k in range(KA):
                    src = y_s[:, k * P:(k + 1) * P] if t == 8 else y_tile(t)[:, k * P:(k + 1) * P]
                    ins = pe.transpose(slot[2 + t % 2][:, k * P:k * P + rows(t)], src, ident[0:rows(t), 0:rows(t)])
                full(ins, ("YT", t))

            for t in GLU_TILES[0]:
                turn_y(t)
            pe.wait_ge(ld["wglu"], 16)

            def sum_squares(n):
                c0, c1 = CHUNKS[n]
                pe.wait_ge(sq_ready, 4 * (n + 1))
                fill(pe, ("SS", n), 5)
                for t in range(c0 // P, (c1 + P - 1) // P):
                    for k in range(KA):
                        ins = pe.matmul(slot[5][0:rows(t), t:t + 1], sq[:, k, t * P - c0:t * P - c0 + rows(t)], ones_col, start=(k == 0), stop=(k == KA - 1))
                full(ins, ("SS", n))

            for n, (c0, c1) in enumerate(CHUNKS):
                for t in (3, 2) if n == 0 else (7, 6) if n == 1 else (8,):
                    slots.wait_empty(pe, ("YT", t))
                for m in range(KA):
                    fill(pe, ("Z", n, m), m % 2)
                    for k in range(KA):
                        ins = pe.matmul(slot[m % 2][:, 0:c1 - c0], w_glu[:, k, m * P:(m + 1) * P], yT[:, k, c0:c1], start=(k == 0), stop=(k == KA - 1))
                    full(ins, ("Z", n, m))
                    if m == 0 and n:
                        sum_squares(n - 1)
                for t in GLU_TILES[1] if n == 0 else ():
                    turn_y(t)
            sum_squares(len(CHUNKS) - 1)
            pe.wait_ge(ld["wq"], 16)
            for w in range(2):
                for n, (c0, c1) in enumerate(CHUNKS):
                    for j in range(KA):
                        b = 2 + j % 2
                        fill(pe, ("QK"[w], n, j), b)
                        for k in range(KD):
                            ins = pe.matmul(slot[b][:, 0:c1 - c0], w_q[:, k, w * DA + j * P:w * DA + (j + 1) * P], hT[:, k, c0:c1], start=(k == 0), stop=(k == KD - 1))
                        full(ins, ("QK"[w], n, j))
            for n, (c0, c1) in enumerate(CHUNKS):
                fill(pe, ("F", n), 4 + n % 2)
                for k in range(KD):
                    ins = pe.matmul(slot[4 + n % 2][0:H, 0:c1 - c0], w_q[:, k, 3 * DA:3 * DA + H], hT[:, k, c0:c1], start=(k == 0), stop=(k == KD - 1))
                full(ins, ("F", n))
            slots.wait_empty(pe, ("K", 2, 3))
            for t in range(NT):
                fill(pe, ("V", t), 2 + t % 2)
                for k in range(KD):
                    ins = pe.matmul(slot[2 + t % 2][0:rows(t), :], hT[:, k, t * P:t * P + rows(t)], w_q[:, k, 2 * DA:3 * DA], start=(k == 0), stop=(k == KD - 1))
                full(ins, ("V", t))
                fill(pe, ("KT", t), t % 2)
                for j in range(KA):
                    ins = pe.transpose(slot[t % 2][0:rows(t), j * P:(j + 1) * P], kT[:, j, t * P:t * P + rows(t)], ident)
                full(ins, ("KT", t))
            pe.wait_ge(fg_ready, 1)
            fill(pe, "LF", 4)
            for t in range(NT):
                ins = pe.transpose(slot[4][0:rows(t), t * H:(t + 1) * H], lf[:, t * P:t * P + rows(t)], ident[0:H, 0:H])
                if t < 8:
                    ins = pe.transpose(slot[4][:, P + t * H:P + (t + 1) * H], c_row[:, t * P:(t + 1) * P], ident[0:H, 0:H])
            full(ins, "LF")

            def spread_sums(h, s_):
                fill(pe, ("CB", h), s_)
                for n in range(2):
                    ins = pe.matmul(slot[s_][:, n * 512:(n + 1) * 512], ident[0:H, h:h + 1].to_broadcast([H, P]), c_row[:, n * 512:(n + 1) * 512], start=True, stop=True)
                full(ins, ("CB", h))

            spread_sums(0, 0)
            slots.wait_empty(pe, ("V", 7))

            def logits(it):
                i, h = ATT[it]
                fill(pe, ("L", it), it % 2)
                for c0 in range(0, (i + 1) * P, 512):
                    c1 = min(c0 + 512, (i + 1) * P)
                    ins = pe.matmul(slot[it % 2][:, c0:c1], qT[:, h, i * P:(i + 1) * P], kT[:, h // 2, c0:c1], start=True, stop=True)
                full(ins, ("L", it))

            def weigh(it):
                i, h = ATT[it]
                fill(pe, ("O", it), 4 + it % 2)
                for j in range(i + 1):
                    if j % 4 == 0:
                        slots.wait_empty(pe, ("PT", it, j))
                    ins = pe.matmul(slot[4 + it % 2][:, 0:DH], pt[:, it % 2, j * P:(j + 1) * P], v[:, j, h * DH:(h + 1) * DH], start=(j == 0), stop=(j == i))
                full(ins, ("O", it))

            logits(0)
            logits(1)
            for it, (i, h) in enumerate(ATT):
                if it + 2 < len(ATT):
                    logits(it + 2)
                if i == CB_AT and h + 1 < H:
                    spread_sums(h + 1, (it + 3) % 2)
                pe.wait_ge(p_ready, it + 1)
                for q0 in pt_keys(it):
                    b = 2 + (q0 // 4)
                    fill(pe, ("PT", it, q0), b)
                    for j in range(q0, min(q0 + 4, i + 1)):
                        ins = pe.transpose(slot[b][:, (j - q0) * P:(j - q0 + 1) * P], pr[:, it % 2, j * P:(j + 1) * P], ident)
                    full(ins, ("PT", it, q0))
                if it:
                    weigh(it - 1)
            weigh(len(ATT) - 1)
            pe.wait_ge(ld_lfp, 16 * NSEQ * PAGES)
            fill(pe, "LFP", 2)
            for j in range(PAGES):
                ins = pe.transpose(slot[2][0:NS, j * PAGE:(j + 1) * PAGE], lf_pages[:, j, :], ident)
            full(ins, "LFP")

            def turn_keys(b):
                pe.wait_ge(ld_page[b % 2], 16 * PAGES * (b // 2 + 1))
                for j in range(KA):
                    s_, at = ((1, 0), (1, PAST), (2, 0), (3, 0))[j]
                    if j != 1:
                        fill(pe, ("SK", b, j), s_)
                    for m in range(PAGES):
                        ins = pe.transpose(slot[s_][:, at + m * PAGE:at + (m + 1) * PAGE], kpg[:, b % 2, m, j * P:(j + 1) * P], ident)
                    if j:
                        full(ins, ("SK", b, 0 if j == 1 else j))

            def add_rows(b):
                slots.wait_empty(pe, ("SO", b))
                if b == 0:
                    fill(pe, "SR", 5)
                ins = pe.matmul(slot[5][0:NS, :], sel_row[:, 56 - CH * b:56 - CH * b + NS], o_masked[:, :], start=(b == 0), stop=(b == NSEQ - 1))
                if b < NSEQ - 1:
                    ins.then_inc(smp_om, 1)
                else:
                    full(ins, "SR")

            turn_keys(0)
            pe.wait_ge(smp_c, 1)
            pe.wait_ge(smp_q, 1)
            pe.wait_ge(smp_sel, 1)
            for b in range(NSEQ):
                slots.wait_empty(pe, ("SK", b, 0))
                slots.wait_empty(pe, ("SK", b, 2))
                slots.wait_empty(pe, ("SK", b, 3))
                fill(pe, ("SL", b), 0)
                for j in range(KA):
                    pe.matmul(slot[0][0:NS, 0:PAST], q_bd[:, b, j, :], k_ts[:, b % 2, j, :], start=(j == 0), stop=False)
                pe.matmul(slot[0][0:NS, 0:PAST], sel_seq[:, b, :], c_s[:, 0:PAST], start=False, stop=True)
                for j in range(KA):
                    pe.matmul(slot[0][0:NS, PAST:PAST + CH], q_bd[:, b, j, :], kT[:, j, SEQ + b * CH:SEQ + (b + 1) * CH], start=(j == 0), stop=False)
                ins = pe.matmul(slot[0][0:NS, PAST:PAST + CH], sel_seq[:, b, :], c_s[:, PAST:PAST + CH], start=False, stop=True)
                full(ins, ("SL", b))
                fill(pe, ("SC", b), 4)
                full(pe.matmul(slot[4][0:NS, 0:CH], sel_seq[:, b, :], c_s[:, PAST:PAST + CH], start=True, stop=True), ("SC", b))
                if b:
                    add_rows(b - 1)
                if b + 1 < NSEQ:
                    turn_keys(b + 1)
                pe.wait_ge(smp_p, b + 1)
                fill(pe, ("SP", b), 3)
                for m in range(PAGES):
                    pe.transpose(slot[3][:, m * NS:(m + 1) * NS], p_s[:, m * PAGE:(m + 1) * PAGE], ident[0:NS, 0:NS])
                full(pe.transpose(slot[3][0:CH, PAGES * NS:(PAGES + 1) * NS], p_s[:, PAST:PAST + CH], ident[0:NS, 0:NS]), ("SP", b))
                slots.wait_empty(pe, ("SP", b))
                pe.wait_ge(ld_vnew[b % 2], 16 * (b // 2 + 1))
                pe.wait_ge(ld_vpage[b % 2], 16 * PAGES * (b // 2 + 1))
                fill(pe, ("SO", b), 2)
                for m in range(PAGES):
                    pe.matmul(slot[2][0:NS, :], p_ts[:, m, :], vpg[:, b % 2, m, :], start=(m == 0), stop=False)
                full(pe.matmul(slot[2][0:NS, :], p_ts[0:CH, PAGES, :], v_new[:, b % 2, :], start=False, stop=True), ("SO", b))
            add_rows(NSEQ - 1)
            pe.wait_ge(gate_ready, 1)
            fill(pe, "G1", 0)
            for k in range(KD):
                ins = pe.transpose(slot[0][:, k * P:(k + 1) * P], mod_t[:, 16 + k, 0:1].to_broadcast([P, P]), ident)
            full(ins, "G1")
            fill(pe, "G1S", 1)
            for k in range(KD):
                ins = pe.transpose(slot[1][0:NS, k * P:(k + 1) * P], gate_s[:, k, :], ident)
            full(ins, "G1S")
            pe.wait_ge(wout_scaled, 1)

            def project_out(t, half):
                fill(pe, ("W", t, half), half)
                for n in range(2):
                    for k in range(KA):
                        lhs = tile_of(oT, t, k) if half else ysT[:, k, t * P:t * P + rows(t)]
                        ins = pe.matmul(slot[half][0:rows(t), n * 512:(n + 1) * 512], lhs, w_out[:, half * KA + k, n * 512:(n + 1) * 512], start=(k == 0), stop=(k == KA - 1))
                full(ins, ("W", t, half))

            project_out(0, 0)
            pe.wait_ge(o_ready, 1)
            for t in range(NT):
                fill(pe, ("OT", t), 2 + t % 2)
                for k in range(KA):
                    ins = pe.transpose(slot[2 + t % 2][:, k * P:k * P + rows(t)], o_tok[0:rows(t), t, k * P:(k + 1) * P], ident[0:rows(t), 0:rows(t)])
                full(ins, ("OT", t))
            slots.wait_empty(pe, ("OT", 7))
            slots.wait_empty(pe, ("OT", 8))
            for t in range(NT):
                if t:
                    project_out(t, 0)
                project_out(t, 1)
            pe.wait_ge(ld["router"], 16)

            def second_norm(t):
                slots.wait_empty(pe, ("X2", t))
                fill(pe, ("H2", t), 1)
                for k in range(KD):
                    ins = pe.transpose(slot[1][0:rows(t), k * P:(k + 1) * P], h2T[:, k, t * P:t * P + rows(t)], ident)
                full(ins, ("H2", t))
                fill(pe, ("R", t), 4)
                for k in range(KD):
                    ins = pe.matmul(slot[4][0:rows(t), 0:E], h2T[:, k, t * P:t * P + rows(t)], w_router[:, k, :], start=(k == 0), stop=(k == KD - 1))
                full(ins, ("R", t))

            def shared_gate_up(t):
                fill(pe, ("GS", t), 2 + t % 2)
                for k in range(KD):
                    ins = pe.matmul(slot[2 + t % 2][0:rows(t), :], h2T[:, k, t * P:t * P + rows(t)], sh_gu[:, k, :], start=(k == 0), stop=(k == KD - 1))
                full(ins, ("GS", t))

            for t in range(NT):
                pe.wait_ge(xn2_ready, t + 1)
                fill(pe, ("X2", t), 0)
                for k in range(KD):
                    ins = pe.transpose(slot[0][:, k * P:k * P + rows(t)], h2_tok[0:rows(t), t % 2, k * P:(k + 1) * P], ident[0:rows(t), 0:rows(t)])
                full(ins, ("X2", t))
                if t:
                    second_norm(t - 1)
                if t == 2:
                    pe.wait_ge(ld_shared, 48)
                if t in (2, 3):
                    shared_gate_up(t - 2)
            second_norm(NT - 1)

            def shared_down(t):
                pe.wait_ge(sh_h, t + 1)
                fill(pe, ("HS", t), 4)
                for k in range(2):
                    ins = pe.transpose(slot[4][:, k * P:k * P + rows(t)], h_row[0:rows(t), t % 2, k * P:(k + 1) * P], ident[0:rows(t), 0:rows(t)])
                full(ins, ("HS", t))
                slots.wait_empty(pe, ("HS", t))
                fill(pe, ("YS2", t), t % 2)
                for n in range(2):
                    for k in range(2):
                        ins = pe.matmul(slot[t % 2][0:rows(t), n * 512:(n + 1) * 512], hTs[:, k, 0:rows(t)], sh_d[:, k, n * 512:(n + 1) * 512], start=(k == 0), stop=(k == 1))
                full(ins, ("YS2", t))

            for s_ in (idx_mm, turned, gu_done, ht_turned, down_done):
                pe.sem_inc(s_, 2)

            def index(b, par):
                pe.wait_ge(onehot_ready, b + 1)
                pe.wait_ge(idx_read, b + 1)
                for i in range(NT):
                    ins = pe.matmul(slot[5][:, 0:5], onehot[:, par, i, :], tok_cols[:, par, i, :], start=(i == 0), stop=(i == NT - 1))
                ins.then_inc(idx_mm, 1)

            for t in range(1, NT):
                if t > 1:
                    shared_gate_up(t)
                shared_down(t - 1)
                if t == 4:
                    pe.wait_ge(routed, 1)
                    fill(pe, "RK", 0)
                    for i in range(NT):
                        for j in range(i + 1):
                            ins = pe.matmul(slot[0][:, i * E:(i + 1) * E], tri if j == i else ones_b, sel_b[:, j, :], start=(j == 0), stop=(j == i))
                    full(ins, "RK")
                    fill(pe, "CN", 5)
                    for i in range(NT):
                        ins = pe.matmul(slot[5][:, 0:E], ones_b, sel_b[:, i, :], start=(i == 0), stop=(i == NT - 1))
                    full(ins, "CN")
                if t == 6:
                    pe.wait_ge(blocks_ready, 1)
                    fill(pe, "BT", 1)
                    for i, col in enumerate((blk_base, blk_expert, blk_ord, blk_ring, ord_expert, ord_release)):
                        ins = pe.transpose(slot[1][:, i * P:(i + 1) * P], col.to_broadcast([P, P]), ident)
                    full(ins, "BT")
            slots.wait_empty(pe, "BT")
            slots.wait_empty(pe, "CN")
            index(0, 0)
            index(1, 1)
            shared_down(NT - 1)
            slots.wait_empty(pe, ("HS", 8))
            slots.wait_empty(pe, ("YS2", 8))
            slots.wait_empty(pe, ("YS2", 7))
            slots.wait_empty(pe, ("GS", 7))
            n_pairs = pe.value_load(n_pairs_t[0:1, 0:1], min_val=1, max_val=MAXPAIR)

            def turn(b, par, gathers):
                pe.wait_ge(gathered[par], gathers * 16)
                pe.wait_ge(xt_copied, b + 1)
                for k in range(KD):
                    ins = pe.transpose(slot[0][:, k * P:(k + 1) * P], x_rows[:, par, k * P:(k + 1) * P], ident)
                ins.then_inc(turned, 1)

            def place(b):
                n = pe.value_load(ord_i[0:1, bass.ds(b, 1)], min_val=0, max_val=E - 1)
                at = bass.ds(pe.value_load(ring_i[0:1, bass.ds(b, 1)], min_val=0, max_val=RING - 1), 1)
                pe.wait_ge(weights_in, n + 1)
                return at

            def gate_up(b, par, at):
                pe.wait_ge(xt_copied, b + 2)
                pe.wait_ge(h_done, b + 1)
                for k in range(KD):
                    ins = pe.matmul(slot[2 + par], xTs[:, par, k, :], ring[:, at, k, :].rearrange("p a n -> p (a n)"), start=(k == 0), stop=(k == KD - 1))
                ins.then_inc(gu_done, 1)

            def turn_h(b, par):
                pe.wait_ge(h_done, b + 3)
                pe.wait_ge(ht_copied, b + 1)
                for k in range(2):
                    ins = pe.transpose(slot[4][:, k * P:(k + 1) * P], h_row[:, par, k * P:(k + 1) * P], ident)
                ins.then_inc(ht_turned, 1)

            turn(0, 0, 1)
            index(2, 0)
            gate_up(0, 0, place(0))
            turn(1, 1, 1)
            turn_h(0, 0)
            index(3, 1)
            with pe.Fori(0, n_pairs) as j:
                for par in range(2):
                    b = j * 2 + par
                    at = bass.ds(pe.value_load(ring_i[0:1, bass.ds(b, 1)], min_val=0, max_val=RING - 1), 1)
                    gate_up(b + 1, 1 - par, place(b + 1))
                    turn(b + 2, par, j + 2)
                    pe.wait_ge(ht_copied, b + 2)
                    pe.wait_ge(y_act, b + 1)
                    pe.wait_ge(y_dve, b + 1)
                    for n in range(2):
                        for k in range(2):
                            ins = pe.matmul(slot[1][:, n * 512:(n + 1) * 512], hTs[:, k, :], ring[:, at, 8 + 2 * k + n, :].rearrange("p a n -> p (a n)"), start=(k == 0), stop=(k == 1))
                    ins.then_inc(down_done, 1)
                    turn_h(b + 1, 1 - par)
                    index(b + 4, par)
            pe.wait_ge(y_act, n_pairs * 2 + 1)
            pe.wait_ge(y_dve, n_pairs * 2 + 1)
            pe.wait_ge(xt_copied, n_pairs * 2 + 3)
            pe.sem_inc(down_done, 2)
            pe.wait_ge(cols_ready, 1)
            for q, (c, src) in enumerate(((40, mod_t), (0, af), (48, mod_t))):
                for smp in range(2):
                    fill(pe, ("FR", q, smp), smp)
                    for k in range(KD):
                        s_ = fin_s_cols[:, q, k, :] if smp else src[:, c + k, 0:1].to_broadcast([P, P])
                        ins = pe.transpose(slot[smp][0:NS if smp else P, k * P:(k + 1) * P], s_, ident)
                    full(ins, ("FR", q, smp))

        @block.vector
        def _(dve):
            full, empty = slots.wait_full, slots.empty
            tt, ts, stt, cp = dve.tensor_tensor, dve.tensor_scalar, dve.scalar_tensor_tensor, dve.tensor_copy

            def cmul(dr, di, ar, ai, br, bi, t, sign=1):
                dlink(tt(t, ai, bi, ALU.mult))
                dlink(tt(dr, ar, br, ALU.mult))
                dlink(tt(dr, dr, t, ALU.subtract))
                dlink(tt(t, ar, bi, ALU.mult))
                dlink(tt(di, ai, br, ALU.mult))
                if sign > 0:
                    dlink(tt(di, di, t, ALU.add))
                else:
                    dlink(stt(di, di, -1.0, t, ALU.mult, ALU.subtract))

            full(dve, "CS")
            empty(cp(cs_t.rearrange("p k m -> p (k m)"), slot[5][:, 0:KD * NM]), "CS")
            full(dve, "T0")
            dlink(cp(pack_t, slot[0][:, 0:100]))
            dlink(cp(prm, slot[0][:, 128:176]))
            empty(cp(d_t, slot[0][0:GI, 192:192 + G]), "T0")
            full(dve, "T1")
            empty(cp(h0_t.rearrange("p r b g -> p (r b g)"), slot[1][:, 0:2 * P]), "T1")
            full(dve, "T2")
            empty(cp(c_l1.rearrange("p r g i -> p (r g i)"), slot[4]), "T2")

            sv = [s5_small[:, i, :] for i in range(24)]
            lr, li = prm[:, 0:16], prm[:, 16:32]
            dt_, mag, m8, mlr, ang, kk, r, r2, sn, cs, f_re, f_im, den, nre, t0, phi, phih, phil, a_re, a_im, t1 = sv[:21]

            def exp_exact(dst, x, k_, e_, r_):
                dlink(ts(r_, x, -87.0, 88.0, ALU.max, ALU.min))
                dlink(ts(k_, r_, 1.0 / np.log(2.0), MAGIC, ALU.mult, ALU.add))
                dlink(ts(k_, k_, -MAGIC, None, ALU.add))
                dlink(stt(r_, k_, -0.693359375, r_, ALU.mult, ALU.add))
                dlink(stt(r_, k_, 2.12194440e-4, r_, ALU.mult, ALU.add))
                dlink(ts(k_, k_, 127.0, 8388608.0, ALU.add, ALU.mult))
                dlink(cp(e_.bitcast(I32), k_))
                dlink(ts(dst, r_, 1.9875691500e-4, 1.3981999507e-3, ALU.mult, ALU.add))
                for c_ in (8.3334519073e-3, 4.1665795894e-2, 1.6666665459e-1, 5.0000001201e-1, 1.0, 1.0):
                    dlink(tt(dst, dst, r_, ALU.mult))
                    dlink(ts(dst, dst, c_, None, ALU.add))
                dlink(tt(dst, dst, e_, ALU.mult))

            exp_exact(dt_, prm[:, 32:48], sv[10], sv[11], sv[12])
            dlink(tt(mlr, lr, dt_, ALU.mult))
            dlink(tt(ang, li, dt_, ALU.mult))
            dlink(ts(kk, ang, 1.0 / TWO_PI, MAGIC, ALU.mult, ALU.add))
            dlink(ts(kk, kk, -MAGIC, None, ALU.add))
            dlink(stt(r, kk, -C1, ang, ALU.mult, ALU.add))
            dlink(stt(r, kk, -C2, r, ALU.mult, ALU.add))
            dlink(ts(r, r, PI_SAFE, -PI_SAFE, ALU.min, ALU.max))
            dlink(ts(r2, r, 0.5 * np.pi, None, ALU.add))
            dlink(ts(t0, r2, PI_SAFE, -TWO_PI, ALU.is_gt, ALU.mult))
            dlink(tt(r2, r2, t0, ALU.add))
            dlink(ts(r2, r2, PI_SAFE, -PI_SAFE, ALU.min, ALU.max))
            dve.sem_inc(s5_angles, 1)
            dlink(cp(sv[21], mlr))
            dlink(ts(sv[22], mlr, float(CH), None, ALU.mult))
            exp_exact(s5_small[:, 1:3], s5_small[:, 21:23], s5_small[:, 10:12], s5_small[:, 12:14], s5_small[:, 18:20])
            dlink(ts(phi, r, 8.0 / TWO_PI, None, ALU.mult))
            dlink(ts(kk, phi, MAGIC, -MAGIC, ALU.add, ALU.add))
            dlink(tt(phi, phi, kk, ALU.subtract))
            dlink(ts(phih, phi, 6144.0, -6144.0, ALU.add, ALU.add))
            dlink(tt(phil, phi, phih, ALU.subtract))
            dve.wait_ge(s5_trig, 1)
            dlink(cp(mag8, m8))
            dlink(tt(a_re, mag, cs, ALU.mult))
            dlink(tt(a_im, mag, sn, ALU.mult))
            dlink(tt(den, lr, lr, ALU.mult))
            dlink(tt(t0, li, li, ALU.mult))
            dlink(tt(den, den, t0, ALU.add))
            dlink(dve.reciprocal(den, den))
            dlink(ts(nre, a_re, -1.0, None, ALU.add))
            dlink(tt(f_re, nre, lr, ALU.mult))
            dlink(tt(t0, a_im, li, ALU.mult))
            dlink(tt(f_re, f_re, t0, ALU.add))
            dlink(tt(f_re, f_re, den, ALU.mult))
            dlink(tt(f_im, a_im, lr, ALU.mult))
            dlink(tt(t0, nre, li, ALU.mult))
            dlink(tt(f_im, f_im, t0, ALU.subtract))
            dlink(tt(f_im, f_im, den, ALU.mult))
            dve.wait_ge(ld["bc"], 32)
            tb = tmp[:, 0:GP * GI].rearrange("p (g i) -> p g i", g=GP)

            def over_i(a, n=GI):
                return a.unsqueeze(2).to_broadcast([P, GP, n])

            cmul(bb[:, 0], bb[:, 1], over_i(f_re), over_i(f_im), b_raw[:, 0], b_raw[:, 1], tb)
            dlink(dve.memset(pw[:, 0, :, 0], 1.0))
            dlink(dve.memset(pw[:, 1, :, 0], 0.0))
            dlink(cp(pw[:, 0, :, 1], a_re))
            dlink(cp(pw[:, 1, :, 1], a_im))
            for lo, n in ((1, 1), (2, 2), (4, 4)):
                src = [pw[:, i, :, 1:1 + n] for i in range(2)]
                by = [over_i(pw[:, i, :, lo], n) for i in range(2)]
                cmul(pw[:, 0, :, lo + 1:lo + 1 + n], pw[:, 1, :, lo + 1:lo + 1 + n], src[0], src[1], by[0], by[1],
                     tmp[:, 0:GP * n].rearrange("p (g n) -> p g n", g=GP))
            for i in range(2):
                dlink(cp(a8[:, i], pw[:, i, :, 8]))
                for n in range(8):
                    dlink(cp(pwr[:, i, :, n], pw[:, i, :, 7 - n]))
            n4 = [P, GP, 9, GI]
            cmul(CP[:, 0], CP[:, 1], c_l1[:, 0].unsqueeze(2).to_broadcast(n4), c_l1[:, 1].unsqueeze(2).to_broadcast(n4),
                 pw[:, 0].unsqueeze(3).to_broadcast(n4), pw[:, 1].unsqueeze(3).to_broadcast(n4),
                 tmp.rearrange("p (g n i) -> p g n i", g=GP, n=9), sign=-1)
            n4 = [P, GP, 8, GI]
            cmul(BP[:, 0], BP[:, 1], bb[:, 0].unsqueeze(2).to_broadcast(n4), bb[:, 1].unsqueeze(2).to_broadcast(n4),
                 pwr[:, 0].unsqueeze(3).to_broadcast(n4), pwr[:, 1].unsqueeze(3).to_broadcast(n4),
                 tmp[:, 0:2048].rearrange("p (g n i) -> p g n i", g=GP, n=8))
            dve.sem_inc(s5_mats, 2)
            n3 = [P, GP, NC_]
            t3 = tmp[:, 0:2048].rearrange("p (g c) -> p g c", g=GP)
            c3 = iota_row.unsqueeze(1).to_broadcast(n3)
            ph, pl = phih.unsqueeze(2).to_broadcast(n3), phil.unsqueeze(2).to_broadcast(n3)
            dlink(tt(Etab[:, 0], c3, ph, ALU.mult))
            dlink(ts(t3, Etab[:, 0], MAGIC, -MAGIC, ALU.add, ALU.add))
            dlink(tt(Etab[:, 0], Etab[:, 0], t3, ALU.subtract))
            dlink(tt(t3, c3, pl, ALU.mult))
            dlink(tt(Etab[:, 1], Etab[:, 0], t3, ALU.add))
            dlink(ts(t3, Etab[:, 1], MAGIC, -MAGIC, ALU.add, ALU.add))
            dlink(tt(Etab[:, 1], Etab[:, 1], t3, ALU.subtract))
            dlink(ts(Etab[:, 0], Etab[:, 1], 0.25, None, ALU.add))
            dlink(ts(t3, Etab[:, 0], MAGIC, -MAGIC, ALU.add, ALU.add))
            dlink(tt(Etab[:, 0], Etab[:, 0], t3, ALU.subtract))
            dlink(ts(Etab[:, 0:2], Etab[:, 0:2], 0.4999999, -0.4999999, ALU.min, ALU.max))
            dve.sem_inc(e_angle, 1)
            dve.wait_ge(mod_done, NADA + NADF)
            for dst, c, g in ((a1, 8, 64), (a2, 32, 72), (af, 56, 80)):
                dlink(ts(dst, mod_t[:, c:c + 8, :], 1.0, None, ALU.add))
                dlink(tt(dst, dst, pack_t[:, g:g + 8].unsqueeze(2).to_broadcast([P, KD, NM]), ALU.mult))
            for q in range(8):
                full(dve, ("BS", q))
                dst = BS[:, 2 * q:2 * q + 2].rearrange("p g a r n -> p g r a n")
                empty(cp(dst, slot[2 + q % 2].rearrange("p (g r a n) -> p g r a n", g=2, r=2, a=2)), ("BS", q))
            for q in range(8):
                full(dve, ("K", q))
                empty(cp(Ksb[:, groups_of(q)[0]:8 * (q // 2 + 1):2, :], slot[4 + q % 2][0:GI, :].rearrange("p (g n) -> p g n", g=4)), ("K", q))
            slots.wait_empty(dve, ("K", 7))
            slots.wait_empty(dve, ("K", 6))
            skip = tmp[0:GI, 0:G * GI].rearrange("p (g i) -> p g i", g=G)
            dlink(tt(skip, ident[0:GI, 0:GI].unsqueeze(1).to_broadcast([GI, G, GI]), d_t.unsqueeze(2).to_broadcast([GI, G, GI]), ALU.mult))
            dlink(tt(Ksb[:, :, 0:GI], Ksb[:, :, 0:GI], skip, ALU.add))
            dve.sem_inc(k_ready, 1)

            def modulate(key, t, src, dst_of, scale, shift):
                full(dve, key)
                if t < 8:
                    for k in range(KD):
                        ins = ts(dst_of(k), src[:, k * P:(k + 1) * P], scale[:, k, 0:1], shift(k)[:, 0:1], ALU.mult, ALU.add)
                    empty(ins, key)
                else:
                    for k in range(KD):
                        v_ = src[:, k * P:k * P + NS].rearrange("p (b s) -> p b s", b=NSEQ)
                        d_ = dst_of(k).rearrange("p (b s) -> p b s", b=NSEQ)
                        dlink(tt(d_, v_, scale[:, k, 1:NM].unsqueeze(2).to_broadcast([P, NSEQ, CH]), ALU.mult))
                        ins = tt(d_, d_, shift(k)[:, 1:NM].unsqueeze(2).to_broadcast([P, NSEQ, CH]), ALU.add)
                        if k < KD - 1:
                            dlink(ins)
                    empty(ins, key)

            for t in range(NT):
                m = rows(t)
                dve.wait_ge(x_sq, t + 1)
                dlink(ts(ssq[0:m, t:t + 1], ssq[0:m, t:t + 1], 1.0 / D, EPS, ALU.mult, ALU.add))
                dve.sem_inc(x_var, 1)
                dve.wait_ge(x_std, t + 1)
                dlink(dve.reciprocal(rstd[0:m, t:t + 1], rstd[0:m, t:t + 1]))
                ts(x_buf[0:m, t % 2, :], x_buf[0:m, t % 2, :], rstd[0:m, t:t + 1], None, ALU.mult).then_inc(xn_ready, 1)
                if t:
                    modulate(("X", t - 1), t - 1, slot[(t - 1) % 2], lambda k, t_=t - 1: tile_of(hT, t_, k), a1, lambda k: mod_t[:, k])
            modulate(("X", 8), 8, slot[0], lambda k: tile_of(hT, 8, k), a1, lambda k: mod_t[:, k])
            full(dve, ("ADA", NADA + NADF - 1))
            for q in range(8):
                full(dve, ("UT", q))
                empty(cp(U[:, 4 * q:4 * q + 4, 0:NC_], slot[4 + q % 2].rearrange("p (g c) -> p g c", g=4)), ("UT", q))
            dve.wait_ge(e_table, 1)
            dlink(dve.memset(Hp[:, :, :, 0:1], 0.0))
            for q in range(4):
                gs = slice(4 * q, 4 * q + 4)
                for gp in range(4 * q + 1, 4 * q + 4):
                    slots.wait_empty(dve, ("S", gp))
                Sr, Si = S[:, 0, gs, 0:NC_], S[:, 1, gs, 0:NC_]
                Hr, Hi = Hp[:, 0, gs, 1:NC_ + 1], Hp[:, 1, gs, 1:NC_ + 1]
                Ec, Es, tq = Etab[:, 0, gs], Etab[:, 1, gs], t3[:, gs]
                dlink(tt(Hr, Sr, Ec, ALU.mult))
                dlink(tt(tq, Si, Es, ALU.mult))
                dlink(tt(Hr, Hr, tq, ALU.add))
                dlink(tt(Hi, Si, Ec, ALU.mult))
                dlink(tt(tq, Sr, Es, ALU.mult))
                dlink(tt(Hi, Hi, tq, ALU.subtract))
                for ri in range(2):
                    for gp in range(4 * q, 4 * q + 4):
                        ins = dve.tensor_tensor_scan(S[:, ri, gp, 0:NC_], mag8[:, gp:gp + 1].to_broadcast([P, NC_]), Hp[:, ri, gp, 1:NC_ + 1], 0.0, ALU.mult, ALU.add)
                dlink(ins)
                dlink(tt(Hr, Sr, Ec, ALU.mult))
                dlink(tt(tq, Si, Es, ALU.mult))
                dlink(tt(Hr, Hr, tq, ALU.subtract))
                dlink(tt(Hi, Sr, Es, ALU.mult))
                dlink(tt(tq, Si, Ec, ALU.mult))
                dlink(tt(Hi, Hi, tq, ALU.add))
                dve.sem_inc(state_ready, 1)
            dlink(cp(fin_p, Hp[:, :, :, NC_]))
            n3 = [P, NSEQ, GP]
            tf = tmp[:, 2048:2048 + NSEQ * GP].rearrange("p (b g) -> p b g", b=NSEQ)
            ar, ai = (a8[:, i].unsqueeze(1).to_broadcast(n3) for i in range(2))
            cmul(fin_s[:, 0], fin_s[:, 1], h0_t[:, 0], h0_t[:, 1], ar, ai, tf)
            for ri in range(2):
                dlink(tt(fin_s[:, ri], fin_s[:, ri], S[:, ri, :, NC_:].rearrange("p g b -> p b g"), ALU.add))
            dve.sem_inc(fin_ready, 1)
            full(dve, "FIN")
            dlink(cp(fin_out[0:GP, 0], slot[0][0:GP, 0:2 * P]))
            empty(cp(fin_out[:, 1], slot[0][:, 512:512 + 2 * P]), "FIN")
            def y_out(t):
                m = rows(t)
                full(dve, ("YT", t))
                empty(cp(yT[:, :, t * P:t * P + m], slot[2 + t % 2].rearrange("p (k c) -> p k c", k=KA)[:, :, 0:m]), ("YT", t))

            for t in GLU_TILES[0]:
                y_out(t)
            slots.wait_empty(dve, ("YT", 7))
            slots.wait_empty(dve, ("YT", 6))
            for n, (c0, c1) in enumerate(CHUNKS):
                for m in range(KA):
                    dve.wait_ge(sig_ready, KA * n + m + 1)
                    tt(ysT[:, m, c0:c1], yT[:, m, c0:c1], sig[:, m % 2, 0:c1 - c0], ALU.mult).then_inc(ys_ready, 1)
                for t in GLU_TILES[1] if n == 0 else ():
                    y_out(t)
                    slots.wait_empty(dve, ("YT", t))
                full(dve, ("SS", n))
                for t in range(c0 // P, (c1 + P - 1) // P):
                    ins = ts(rstd_y[0:rows(t), t:t + 1], slot[5][0:rows(t), t:t + 1], 1.0 / DA, EPS, ALU.mult, ALU.add)
                empty(ins, ("SS", n))
            slots.wait_empty(dve, ("SS", 2))
            dve.sem_inc(ss_copied, 1)
            dve.wait_ge(ss_root, 1)
            dlink(dve.reciprocal(rstd_y, rstd_y))
            for n, (c0, c1) in enumerate(CHUNKS):
                for j in range(KA):
                    full(dve, ("K", n, j))
                    empty(cp(kT[:, j, c0:c1], slot[2 + j % 2][:, 0:c1 - c0]), ("K", n, j))
            dve.wait_ge(ld["fgate"], 16)
            for n, (c0, c1) in enumerate(CHUNKS):
                full(dve, ("F", n))
                empty(ts(lf_a[:, c0:c1], slot[4 + n % 2][0:H, 0:c1 - c0], b_fg[0:H, 0:1], None, ALU.add), ("F", n))
            slots.wait_empty(dve, ("F", 2))
            slots.wait_empty(dve, ("F", 1))
            dlink(stt(lf, lf_a, -1.0, lf_a, ALU.mult, ALU.max))
            dve.sem_inc(fg_step, 1)
            dve.wait_ge(fg_exp, 1)
            dlink(ts(lf_c, lf, 1.0, None, ALU.add))
            dlink(stt(lf, lf_c, -1.0, lf, ALU.add, ALU.subtract))
            dlink(dve.reciprocal(lf_c, lf_c))
            dlink(tt(lf, lf, lf_c, ALU.mult))
            dlink(tt(lf_b, lf_b, lf, ALU.subtract))
            dlink(ts(lf_a, lf_a, 0.0, None, ALU.min))
            dlink(tt(lf, lf_a, lf_b, ALU.subtract))
            for t in range(NT):
                full(dve, ("KT", t))
                if t >= 2:
                    dve.wait_ge(stored_k[t % 2], 16 * (t // 2))
                ins = cp(k_tok[0:rows(t), t % 2, :], slot[t % 2][0:rows(t), 0:DA])
                empty(ins, ("KT", t))
            full(dve, ("V", 8))
            dlink(dve.tensor_tensor_scan(c_row[:, 0:SEQ], ones_col[0:H, :].to_broadcast([H, SEQ]), lf[:, 0:SEQ], 0.0, ALU.mult, ALU.add))
            dve.sem_inc(fg_ready, 1)
            full(dve, "LF")
            dlink(cp(lf_tok, slot[4][:, 0:NT * H]))
            empty(cp(c_tok, slot[4][:, P:P + CH * H]), "LF")
            slots.wait_empty(dve, "LF")
            def one_over_sum(it):
                dve.wait_ge(p_ready, it + 1)
                if it >= 4:
                    slots.wait_empty(dve, ("O", it - 4))
                dve.reciprocal(att_one[:, 4 + it % 4:5 + it % 4], att_one[:, 12 + it % 4:13 + it % 4]).then_inc(recip_ready, 1)

            for it, (i, h) in enumerate(ATT):
                n = (i + 1) * P
                full(dve, ("L", it))
                if i == 0:
                    slots.wait_empty(dve, ("CB", h))
                if it >= 2:
                    dve.wait_ge(p_ready, it - 1)
                sc_ = sc[:, it % 2, :]
                ins = stt(sc_[:, 0:n], slot[it % 2][:, 0:n], c_tok[:, i * H + h:i * H + h + 1], neg_c[h % 2][:, 0:n], ALU.add, ALU.add)
                empty(ins, ("L", it))
                slots.wait_empty(dve, ("L", it))
                dlink(tt(sc_[:, n - P:n], sc_[:, n - P:n], causal, ALU.add))
                dve.tensor_reduce(att_one[:, it % 2:it % 2 + 1], sc_[:, 0:n], AX.X, ALU.max, negate=True).then_inc(s_ready, 1)
                if it:
                    one_over_sum(it - 1)
            one_over_sum(len(ATT) - 1)
            full(dve, "LFP")
            empty(cp(lf_s[:, 0:PAST], slot[2][0:NS, :]), "LFP")
            slots.wait_empty(dve, "LFP")
            dve.wait_ge(lf_moved, 16 * NSEQ)
            dlink(dve.tensor_tensor_scan(c_s, ones_col[0:NS, :].to_broadcast([NS, PAST + CH]), lf_s, 0.0, ALU.mult, ALU.add))
            dlink(ts(c_s, c_s, -1.0, None, ALU.mult))
            dve.sem_inc(smp_c, 1)
            dve.wait_ge(smp_pool, 1)
            dlink(dve.tensor_reduce(same_tok, ident[0:NS, 0:NS].rearrange("p (h s) -> p s h", s=CH), AX.X, ALU.add))
            dlink(tt(s_one, same_tok, iota_row[0:NS, 0:CH], ALU.mult))
            dlink(dve.tensor_reduce(att_one[0:NS, 8:9], s_one, AX.X, ALU.add))
            dlink(ts(new_mask, iota_row[0:NS, 0:CH], att_one[0:NS, 8:9], NEG, ALU.is_gt, ALU.mult))
            dlink(cp(sel_row[:, 56:64], same_tok))
            dve.sem_inc(smp_sel, 1)
            for h in range(H):
                dlink(cp(q_bd[:, :, h // 2, h * CH:(h + 1) * CH], qT[:, h, SEQ:T].rearrange("p (b s) -> p b s", b=NSEQ)))
            dve.sem_inc(smp_q, 1)

            def keys_out(b):
                for j in (2, 3):
                    full(dve, ("SK", b, j))
                    empty(cp(k_ts[:, b % 2, j, :], slot[j]), ("SK", b, j))

            keys_out(0)
            for b in range(NSEQ):
                full(dve, ("SC", b))
                empty(tt(s_one, slot[4][0:NS, 0:CH], same_tok, ALU.mult), ("SC", b))
                slots.wait_empty(dve, ("SC", b))
                dlink(dve.tensor_reduce(att_one[0:NS, 8:9], s_one, AX.X, ALU.add))
                full(dve, ("SL", b))
                if b:
                    full(dve, ("SP", b - 1))
                ins = ts(s_s, slot[0][0:NS, 0:PAST + CH], att_one[0:NS, 8:9], None, ALU.subtract)
                empty(ins, ("SL", b))
                slots.wait_empty(dve, ("SL", b))
                dlink(tt(s_s[:, PAST:], s_s[:, PAST:], new_mask, ALU.add))
                dve.tensor_reduce(att_one[0:NS, 10:11], s_s, AX.X, ALU.max, negate=True).then_inc(smp_s, 1)
                if b + 1 < NSEQ:
                    keys_out(b + 1)
                dve.wait_ge(smp_p, b + 1)
                dlink(dve.reciprocal(att_one[0:NS, 12:13], att_one[0:NS, 11:12]))
                full(dve, ("SO", b))
                if b:
                    dve.wait_ge(smp_om, b)
                empty(stt(o_masked, slot[2][0:NS, :], att_one[0:NS, 12:13], head_mask, ALU.mult, ALU.mult), ("SO", b))
            full(dve, "SR")
            empty(cp(o_tok[0:NS, 8, :], slot[5][0:NS, :]), "SR")
            slots.wait_empty(dve, "SR")
            dlink(cp(gate_s.rearrange("p k (b s) -> p k b s", b=NSEQ), mod_t[:, 16:24, 1:NM].unsqueeze(3).to_broadcast([P, KD, NSEQ, CH])))
            dve.sem_inc(gate_ready, 1)
            slots.wait_empty(dve, ("O", len(ATT) - 1))
            slots.wait_empty(dve, ("O", len(ATT) - 2))
            dve.sem_inc(o_done, 1)
            dve.wait_ge(o_sq, NT)
            dlink(ts(ssq, ssq, 1.0 / DA, EPS, ALU.mult, ALU.add))
            dve.sem_inc(x_var, 1)
            dve.wait_ge(x_std, NT + 1)
            dlink(dve.reciprocal(rstd, rstd))
            for t in range(NT):
                ins = ts(o_tok[0:rows(t), t, :], o_tok[0:rows(t), t, :], rstd[0:rows(t), t:t + 1], None, ALU.mult)
            dlink(ins)
            dve.sem_inc(o_ready, 1)
            dve.wait_ge(ld_res, 32)
            slots.wait_empty(dve, "G1")
            slots.wait_empty(dve, "G1S")
            for t in range(NT):
                m = rows(t)
                mix = h2_tok[0:m, t % 2, :]
                slots.wait_empty(dve, ("W", t, 0))
                full(dve, ("W", t, 1))
                ins = tt(mix, mix, slot[1][0:m, :], ALU.add)
                empty(ins, ("W", t, 1))
                slots.wait_empty(dve, ("W", t, 1))
                dlink(tt(mix, mix, gate_rows[0:m, int(t == 8), :], ALU.mult))
                tt(x1[0:m, t, :], x1[0:m, t, :], mix, ALU.add).then_inc(x1_ready, 1)
            dve.wait_ge(x1_sq, NT)
            dlink(ts(ssq, ssq, 1.0 / D, EPS, ALU.mult, ALU.add))
            dve.sem_inc(x_var, 1)
            dve.wait_ge(x_std, NT + 2)
            dlink(dve.reciprocal(rstd, rstd))
            dve.sem_inc(rstd2_ready, 1)
            for t in range(NT):
                modulate(("X2", t), t, slot[0], lambda k, t_=t: h2T[:, k, t_ * P:t_ * P + rows(t_)], a2, lambda k: mod_t[:, 24 + k])
            dve.wait_ge(scores_ready, 1)
            dve.wait_ge(ld_rb, 16)
            dve.wait_ge(pad_scores, 1)
            dlink(tt(biased, scores, r_bias.unsqueeze(1).to_broadcast([P, NT, E]), ALU.add))
            for t in range(NT):
                for g in range(8):
                    ins = dve.max(sort8[:, t, g, :], biased[:, t, g * 8:(g + 1) * 8])
            dlink(ins)
            dlink(tt(g_score, sort8[:, :, :, 0], sort8[:, :, :, 1], ALU.add))
            for t in range(NT):
                ins = dve.max(top8[:, t, :], g_score[:, t, :])
            dlink(ins)
            dlink(dve.memset(top8[:, :, TOPG:8], 3e38))
            for t in range(NT):
                ins = dve.match_replace(g_left[:, t, :], top8[:, t, :], g_score[:, t, :], 2e38)
            dlink(ins)
            dlink(tt(g_left, g_left, g_score, ALU.not_equal))
            gm = g_left.unsqueeze(3).to_broadcast([P, NT, 8, 8])
            b4 = biased.rearrange("p t (g e) -> p t g e", g=8)
            w4 = masked.rearrange("p t (g e) -> p t g e", g=8)
            dlink(tt(w4, b4, gm, ALU.mult))
            dlink(ts(g_left, g_left, 1e30, -1e30, ALU.mult, ALU.add))
            dlink(tt(w4, w4, gm, ALU.add))
            for t in range(NT):
                ins = dve.max(top8[:, t, :], masked[:, t, :])
            dlink(ins)
            dlink(dve.memset(top8[:, :, TOPK:8], 3e38))
            for t in range(NT):
                ins = dve.match_replace(sel_f[:, t, :], top8[:, t, :], masked[:, t, :], 2e38)
            dlink(ins)
            dlink(tt(sel_f, sel_f, masked, ALU.not_equal))
            dlink(dve.memset(sel_f[NS:P, 8, :], 0.0))
            dlink(cp(sel_b, sel_f))
            dve.sem_inc(routed, 1)
            dlink(tt(scores, scores, sel_f, ALU.mult))
            dlink(dve.tensor_reduce(denom, scores, AX.X, ALU.add))
            dlink(dve.memset(denom[NS:P, 8:9], 1.0))
            dlink(dve.reciprocal(denom, denom))
            dlink(tt(scores, scores, denom.unsqueeze(2).to_broadcast([P, NT, E]), ALU.mult))
            dlink(ts(scores, scores, SCALE_ROUTED, None, ALU.mult))
            dlink(cp(tok_all[:, :, :, 0], iota_part.unsqueeze(1).to_broadcast([P, NT, E])))
            dlink(ts(tok_all[:, :, :, 0], tok_all[:, :, :, 0], 1.0, None, ALU.add))
            dlink(cp(tok_all[:, :, :, 1], iota_row[:, 0:NT].unsqueeze(2).to_broadcast([P, NT, E])))
            dlink(cp(tok_all[:, :, :, 2], scores))
            dlink(tt(scores, scores, tok_all[:, :, :, 2], ALU.subtract))
            dlink(cp(tok_all[:, :, :, 3], scores))
            dlink(tt(scores, scores, tok_all[:, :, :, 3], ALU.subtract))
            dlink(cp(tok_all[:, :, :, 4], scores))
            full(dve, "RK")
            rk = slot[0][:, 0:NT * E].rearrange("p (t e) -> p t e", t=NT)
            empty(tt(rank, rk, sel_f, ALU.mult), "RK")
            slots.wait_empty(dve, "RK")
            dlink(ts(sel_f, sel_f, -1.0, None, ALU.add))
            dlink(tt(rank, rank, sel_f, ALU.add))
            full(dve, "CN")
            empty(cp(cnt, slot[5][:, 0:E]), "CN")
            slots.wait_empty(dve, "CN")
            dlink(ts(nblk, cnt, 0.0, None, ALU.is_gt))
            for i in range(1, NT):
                dlink(stt(nblk, cnt, float(P * i), nblk, ALU.is_gt, ALU.add))
            dlink(dve.tensor_tensor_scan(ends, ones_col.to_broadcast([P, E]), nblk, 0.0, ALU.mult, ALU.add))
            dlink(ts(below, ends, iota_part[:, 0:1], None, ALU.is_le))
            dlink(dve.tensor_reduce(blk_expert, below, AX.X, ALU.add))
            dlink(tt(below, below, nblk, ALU.mult))
            dlink(dve.tensor_reduce(blk_base, below, AX.X, ALU.add))
            dlink(tt(blk_base, iota_part, blk_base, ALU.subtract))
            dlink(ts(blk_base, blk_base, float(P), None, ALU.mult))
            dlink(ts(blk_tmp, iota_part, ends[:, E - 1:E], 65536.0, ALU.is_ge, ALU.mult))
            dlink(tt(blk_base, blk_base, blk_tmp, ALU.add))
            dlink(ts(blk_expert, blk_expert, float(E - 1), None, ALU.min))
            dlink(ts(filled_experts, nblk, 0.0, None, ALU.is_gt))
            dlink(ts(below, ends, iota_part[:, 0:1], None, ALU.is_le))
            dlink(tt(below, below, filled_experts, ALU.mult))
            dlink(dve.tensor_reduce(blk_ord, below, AX.X, ALU.add))
            dlink(dve.tensor_reduce(blk_tmp, filled_experts, AX.X, ALU.add))
            dlink(ts(blk_tmp, blk_tmp, -1.0, None, ALU.add))
            dlink(tt(blk_ord, blk_ord, blk_tmp, ALU.min))
            dlink(ts(blk_ring, blk_ord, -0.5 * (RING - 1), 1.0 / RING, ALU.add, ALU.mult))
            dlink(ts(blk_ring, blk_ring, MAGIC, -MAGIC, ALU.add, ALU.add))
            dlink(stt(blk_ring, blk_ring, float(RING), blk_ord, ALU.mult, ALU.subtract))
            dlink(ts(blk_ring, blk_ring, float(RING - 1), None, ALU.add))
            dlink(dve.tensor_tensor_scan(cnt, ones_col.to_broadcast([P, E]), filled_experts, 0.0, ALU.mult, ALU.add))
            dlink(ts(below, cnt, iota_part[:, 0:1], None, ALU.is_le))
            dlink(dve.tensor_reduce(ord_expert, below, AX.X, ALU.add))
            dlink(ts(ord_expert, ord_expert, float(E - 1), None, ALU.min))
            dlink(ts(blk_tmp, iota_part, float(1 - RING), None, ALU.add))
            dlink(ts(below, cnt, blk_tmp[:, 0:1], None, ALU.is_le))
            dlink(tt(below, below, nblk, ALU.mult))
            dlink(dve.tensor_reduce(ord_release, below, AX.X, ALU.add))
            dlink(ts(blk_tmp, ord_release, ends[:, E - 1:E], 2.0, ALU.is_equal, ALU.mult))
            dlink(ts(ord_release, ord_release, 2.0, None, ALU.add))
            dlink(tt(ord_release, ord_release, blk_tmp, ALU.add))
            dlink(ts(blk_tmp, ends[:, E - 1:E], 0.5, 0.25, ALU.mult, ALU.add))
            dlink(ts(blk_tmp, blk_tmp, MAGIC, -MAGIC, ALU.add, ALU.add))
            dlink(cp(n_pairs_t, blk_tmp[0:1, :]))
            dve.sem_inc(blocks_ready, 1)
            full(dve, "BT")
            dlink(cp(base_t, slot[1][:, 0:P]))
            for i, row in enumerate((expert_i, ord_i, ring_i, order_i, release_i)):
                ins = cp(row, slot[1][0:1, (i + 1) * P:(i + 2) * P])
            empty(ins, "BT")
            slots.wait_empty(dve, "BT")
            dlink(ts(pad_row, iota_part, float(T), None, ALU.add))
            dlink(dve.memset(y_zero, 0.0))
            dve.sem_inc(table_ready, 4)
            for s_, n in ((idx_read, 1), (h_done, 2), (ht_copied, 1), (y_dve, 1)):
                dve.sem_inc(s_, n)
            n_pairs = dve.value_load(n_pairs_t[0:1, 0:1], min_val=1, max_val=MAXPAIR)
            loop_step = [0]

            def rlink(ins, s_, val):
                ins.then_inc(s_, 1)
                dve.wait_ge(s_, val)

            def rank_rows(b, par):
                e = dve.value_load(expert_i[0:1, bass.ds(b, 1)], min_val=0, max_val=E - 1)
                dve.wait_ge(idx_mm, b + 1)
                rlink(ts(blk_rank[:, par], rank[:, :, bass.ds(e, 1)].rearrange("p t e -> p (t e)"), base_t[:, bass.ds(b, 1)], None, ALU.subtract), rank_step, b + 1)
                cp(tok_cols[:, par], tok_all[:, :, bass.ds(e, 1), :].rearrange("p t a c -> p t (a c)"))
                tt(onehot[:, par], iota_row.unsqueeze(1).to_broadcast([P, NT, P]), blk_rank[:, par].unsqueeze(2).to_broadcast([P, NT, P]), ALU.is_equal).then_inc(onehot_ready, 1)

            def slot_index(b, par):
                dve.wait_ge(idx_mm, b + 3)
                rlink(cp(slot_cols[:, par], slot[5][:, 0:5]), idx_read, b + 2)
                dve.wait_ge(turned, b + 1)
                i0 = b * 5
                rlink(ts(slot_v[:, 0:1], slot_cols[:, par, 0:1], 1.0, None, ALU.min), slot_step, i0 + 1)
                rlink(stt(slot_v[:, 1:2], slot_cols[:, par, 1:2], float(P), slot_cols[:, par, 0:1], ALU.mult, ALU.add), slot_step, i0 + 2)
                rlink(tt(slot_v[:, 1:2], slot_v[:, 1:2], slot_v[:, 0:1], ALU.subtract), slot_step, i0 + 3)
                cp(g_idx[:, par:par + 1], slot_v[:, 1:2])
                rlink(ts(slot_v[:, 0:1], slot_v[:, 0:1], -1.0, 1.0, ALU.mult, ALU.add), slot_step, i0 + 4)
                stt(row_all[:, bass.ds(b, 1)], slot_v[:, 0:1], pad_row[:, 0:1], slot_v[:, 1:2], ALU.mult, ALU.add)
                rlink(tt(slot_v[:, 2:3], slot_cols[:, par, 2:3], slot_cols[:, par, 3:4], ALU.add), slot_step, i0 + 5)
                tt(w_all[:, bass.ds(b, 1)], slot_v[:, 2:3], slot_cols[:, par, 4:5], ALU.add).then_inc(idx_done, 1)

            def hidden(b, par):
                dve.wait_ge(g_done, b + 1)
                dve.wait_ge(ht_turned, b + 1)
                tt(h_row[:, par, :], e_g[:, par, :], slot[2 + par][:, FE:2 * FE], ALU.mult).then_inc(h_done, 1)

            def hidden_out(b):
                dve.wait_ge(ht_turned, b + 3)
                dve.wait_ge(down_done, b + 2)
                cp(hTs.rearrange("p k c -> p (k c)"), slot[4][:, 0:2 * P]).then_inc(ht_copied, 1)

            rank_rows(0, 0)
            rank_rows(1, 1)
            slot_index(0, 0)
            slot_index(1, 1)
            rank_rows(2, 0)
            slot_index(2, 0)
            rank_rows(3, 1)
            hidden(0, 0)
            hidden_out(0)
            slot_index(3, 1)
            rank_rows(4, 0)
            dve.wait_ge(shared_stored, 1)
            with dve.Fori(0, n_pairs) as j:
                for par in range(2):
                    b = j * 2 + par
                    hidden(b + 1, 1 - par)
                    rank_rows(b + 5, 1 - par)
                    dve.wait_ge(scatter_done, b + 1)
                    rlink(cp(s_idx[:, par:par + 1], row_all[:, bass.ds(b, 1)]), row_step, b + 1)
                    dve.wait_ge(down_done, b + 3)
                    ts(y_buf[:, par, 512:D], slot[1][:, 512:D], w_all[:, bass.ds(b, 1)], None, ALU.mult).then_inc(y_dve, 1)
                    hidden_out(b + 1)
                    dve.wait_ge(y_act, b + 2)
                    slot_index(b + 4, par)
            dve.wait_ge(down_done, n_pairs * 2 + 2)
            dve.wait_ge(weights_in, E)
            for q, src in enumerate((mod_t[:, 40:48, 1:NM], af[:, :, 1:NM], mod_t[:, 48:56, 1:NM])):
                dlink(cp(fin_s_cols[:, q].rearrange("p k (b s) -> p k b s", b=NSEQ), src.unsqueeze(3).to_broadcast([P, KD, NSEQ, CH])))
            dve.sem_inc(cols_ready, 1)
            dve.wait_ge(rows_ready, 1)
            for t in range(NT + 2):
                if t < NT:
                    m, s_ = rows(t), int(t == 8)
                    dve.wait_ge(ld_y[t], 16)
                    dlink(tt(y_rows[0:m, t, :], y_rows[0:m, t, :], fin_rows[0:m, s_, :], ALU.mult))
                    tt(x1[0:m, t, :], x1[0:m, t, :], y_rows[0:m, t, :], ALU.add).then_inc(x2_ready, 1)
                if 1 <= t <= NT:
                    m = rows(t - 1)
                    dve.wait_ge(x2_sq, t)
                    ts(ssq[0:m, t - 1:t], ssq[0:m, t - 1:t], 1.0 / D, EPS, ALU.mult, ALU.add).then_inc(x_var, 1)
                if t >= 2:
                    i = t - 2
                    m, s_ = rows(i), int(i == 8)
                    dve.wait_ge(x_std, NT + 3 + i)
                    dlink(dve.reciprocal(rstd[0:m, i:i + 1], rstd[0:m, i:i + 1]))
                    stt(x1[0:m, i, :], x1[0:m, i, :], rstd[0:m, i:i + 1], fin_rows[0:m, 2 + s_, :], ALU.mult, ALU.mult).then_inc(y_scaled, 1)

        @block.scalar
        def _(act):
            full, empty = slots.wait_full, slots.empty
            f = act.activation
            act.wait_ge(ld["cond"], 32)
            alink(f(cond_act, cond, ACT.Silu))
            act.sem_inc(cs_ready, 1)
            sv = [s5_small[:, i, :] for i in range(24)]
            r, r2, sn, cs = sv[6:10]
            act.wait_ge(s5_angles, 1)
            alink(f(sn, r, ACT.Sin))
            f(cs, r2, ACT.Sin).then_inc(s5_trig, 1)

            def mod_out(n):
                full(act, ("ADT", n))
                for i in range(4):
                    c = 4 * n + i
                    ins = f(mod_t[:, c, :], slot[4 + n % 2][:, i * NM:(i + 1) * NM], ACT.Identity, bias=pack_t[:, c:c + 1])
                    ins.then_inc(slots.drained[4 + n % 2] if i == 3 else act_step, 1)
                    if i < 3:
                        steps["act"] += 1
                act.wait_ge(slots.drained[4 + n % 2], slots.use[("ADT", n)][1])
                act.sem_inc(mod_done, 1)

            for n in range(NADA + NADF):
                full(act, ("ADA", n))
                if n >= 2:
                    full(act, ("ADT", n - 2))
                empty(f(mod_row[:, n % 2, :], slot[2 + n % 2][0:NM, :], ACT.Copy), ("ADA", n))
                if n:
                    mod_out(n - 1)
            mod_out(NADA + NADF - 1)
            act.wait_ge(e_angle, 1)
            alink(f(Etab[:, 0], Etab[:, 0], ACT.Sin, scale=TWO_PI))
            f(Etab[:, 1], Etab[:, 1], ACT.Sin, scale=TWO_PI).then_inc(e_table, 1)

            def u_out(t):
                full(act, ("U", t))
                src = slot[2 + t % 2]
                if t < 8:
                    if t == 0:
                        act.wait_ge(toeplitz, 16 * CH)
                    empty(f(u[:, :, t, :], src.rearrange("p (g i) -> p g i", g=G), ACT.Copy), ("U", t))
                else:
                    empty(f(u_s, src[0:NS, :], ACT.Copy), ("U", t))

            act.wait_ge(ones_set, 1)
            for t in range(NT):
                m = rows(t)
                act.wait_ge(ld_x[t % 2], 16 * (t // 2 + 1))
                f(sq_junk[0:m, :], x_buf[0:m, t % 2, :], ACT.Square, accum_out=ssq[0:m, t:t + 1]).then_inc(x_sq, 1)
                act.wait_ge(x_var, t + 1)
                f(rstd[0:m, t:t + 1], ssq[0:m, t:t + 1], ACT.Sqrt).then_inc(x_std, 1)
                if t >= 2:
                    u_out(t - 2)
            u_out(NT - 2)
            u_out(NT - 1)
            full(act, "UTS")
            empty(f(U[:, :, NC_:], slot[2][:, 0:G * NSEQ].rearrange("p (g b) -> p g b", g=G), ACT.Copy), "UTS")
            full(act, ("U", 8))
            for gp in range(GP):
                full(act, ("S", gp))
                b = (0, 1, 3)[gp % 3]
                empty(f(S[:, :, gp, :], slot[b][:, 0:272].rearrange("p (r c) -> p r c", r=2), ACT.Copy), ("S", gp))
            for q in range(8):
                for smp in range(2):
                    full(act, ("Y", q, smp))
                    b = (2 + q % 2) if not smp else (4 + q % 2)
                    m = NSEQ if smp else P
                    dst = (y8 if smp else y)[:, :, groups_of(q)[0]:8 * (q // 2 + 1):2, :].rearrange("p t g i -> p g t i")
                    empty(f(dst, slot[b][0:m, :].rearrange("p (g t i) -> p g t i", g=4, t=CH), ACT.Gelu_apprx_tanh), ("Y", q, smp))
            slots.wait_empty(act, "T0")
            for n, (c0, c1) in enumerate(CHUNKS):
                for m in range(KA):
                    i = KA * n + m
                    full(act, ("Z", n, m))
                    if i >= 2:
                        act.wait_ge(ys_ready, i - 1)
                    ins = f(sig[:, m % 2, 0:c1 - c0], slot[m % 2][:, 0:c1 - c0], ACT.Sigmoid, bias=pack_t[:, 88 + m:89 + m])
                    ins.then_inc(sig_ready, 1)
                    act.wait_ge(sig_ready, i + 1)
                    act.sem_inc(slots.drained[m % 2], 1)
                    if m:
                        square_y(act, i - 1)
                square_y(act, KA * n + KA - 1)
            act.wait_ge(ss_copied, 1)
            f(rstd_y, rstd_y, ACT.Sqrt).then_inc(ss_root, 1)
            act.wait_ge(q_zero, 1)
            for n, (c0, c1) in enumerate(CHUNKS):
                for j in range(KA):
                    full(act, ("Q", n, j))
                    src = slot[2 + j % 2]
                    for a in range(2):
                        ins = f(qT[a * DH:(a + 1) * DH, 2 * j + a, c0:c1], src[a * DH:(a + 1) * DH, 0:c1 - c0], ACT.Copy, scale=DH ** -0.5)
                    empty(ins, ("Q", n, j))
            act.wait_ge(fg_step, 1)
            alink(f(lf, lf, ACT.Exp, scale=-1.0))
            f(lf_b, lf, ACT.Ln, bias=1.0).then_inc(fg_exp, 1)
            for t in range(NT):
                full(act, ("V", t))
                empty(f(v[0:rows(t), t, :], slot[2 + t % 2][0:rows(t), :], ACT.Copy), ("V", t))
            def spread_out(h):
                full(act, ("CB", h))
                if h >= 2:
                    act.wait_ge(s_ready, 8 * (h - 1))
                empty(f(neg_c[h % 2], slot[slots.use[("CB", h)][0]], ACT.Copy, scale=-1.0), ("CB", h))

            def exponentials(it):
                n = (ATT[it][0] + 1) * P
                act.wait_ge(s_ready, it + 1)
                if it >= 2:
                    full(act, ("PT", it - 2, pt_keys(it - 2)[-1]))
                if it >= 4:
                    act.wait_ge(recip_ready, it - 3)
                f(pr[:, it % 2, 0:n], sc[:, it % 2, 0:n], ACT.Exp, bias=att_one[:, it % 2:it % 2 + 1],
                  accum_out=att_one[:, 12 + it % 4:13 + it % 4]).then_inc(p_ready, 1)

            def attention_out(it):
                i, h = ATT[it]
                full(act, ("O", it))
                act.wait_ge(recip_ready, it + 1)
                empty(f(o_tok[:, i, h * DH:(h + 1) * DH], slot[4 + it % 2][:, 0:DH], ACT.Copy, scale=att_one[:, 4 + it % 4:5 + it % 4]), ("O", it))

            spread_out(0)
            for it, (i, h) in enumerate(ATT):
                exponentials(it)
                for q0 in pt_keys(it):
                    w = min(4, i + 1 - q0) * P
                    full(act, ("PT", it, q0))
                    if it >= 2:
                        full(act, ("O", it - 2))
                    empty(f(pt[:, it % 2, q0 * P:q0 * P + w], slot[2 + q0 // 4][:, 0:w], ACT.Copy), ("PT", it, q0))
                if it:
                    attention_out(it - 1)
                if i == CB_AT and h + 1 < H:
                    spread_out(h + 1)
            attention_out(len(ATT) - 1)
            def keys_out(b):
                full(act, ("SK", b, 0))
                if b == 0:
                    full(act, ("O", len(ATT) - 1))
                if b >= 2:
                    full(act, ("SL", b - 2))
                empty(f(k_ts[:, b % 2, 0:2, :].rearrange("p k n -> p (k n)"), slot[1], ACT.Copy), ("SK", b, 0))

            keys_out(0)
            for b in range(NSEQ):
                act.wait_ge(smp_s, b + 1)
                if b:
                    slots.wait_empty(act, ("SO", b - 1))
                f(p_s, s_s, ACT.Exp, bias=att_one[0:NS, 10:11], accum_out=att_one[0:NS, 11:12]).then_inc(smp_p, 1)
                if b + 1 < NSEQ:
                    keys_out(b + 1)
                full(act, ("SP", b))
                if b:
                    full(act, ("SO", b - 1))
                alink(f(p_ts[:, 0:PAGES, :], slot[3][:, 0:PAGES * NS].rearrange("p (m n) -> p m n", m=PAGES), ACT.Copy))
                empty(f(p_ts[0:CH, PAGES, :], slot[3][0:CH, PAGES * NS:(PAGES + 1) * NS], ACT.Copy), ("SP", b))
            full(act, "G1")
            empty(f(gate_rows[:, 0, :], slot[0], ACT.Copy), "G1")
            full(act, "G1S")
            empty(f(gate_rows[0:NS, 1, :], slot[1][0:NS, :], ACT.Copy), "G1S")
            act.wait_ge(o_done, 1)
            for t in range(NT):
                m = rows(t)
                if t:
                    act.wait_ge(o_sq, t)
                f(sq_o[0:m, :], o_tok[0:m, t, :], ACT.Square, accum_out=ssq[0:m, t:t + 1]).then_inc(o_sq, 1)
            act.wait_ge(x_var, NT + 1)
            f(rstd, ssq, ACT.Sqrt).then_inc(x_std, 1)
            for t in range(NT):
                m = rows(t)
                full(act, ("OT", t))
                src = slot[2 + t % 2].rearrange("p (k c) -> p k c", k=KA)[:, :, 0:m]
                empty(f(oT[:, :, t * P:t * P + m], src, ACT.Copy), ("OT", t))
            for t in range(NT):
                m = rows(t)
                full(act, ("W", t, 0))
                if t >= 2:
                    act.wait_ge(x1_ready, t - 1)
                empty(f(h2_tok[0:m, t % 2, :], slot[0][0:m, :], ACT.Copy, scale=rstd_y[0:m, t:t + 1]), ("W", t, 0))
            for t in range(NT):
                act.wait_ge(x1_ready, t + 1)
                if t:
                    act.wait_ge(x1_sq, t)
                m = rows(t)
                f(sq_x1[0:m, :], x1[0:m, t, :], ACT.Square, accum_out=ssq[0:m, t:t + 1]).then_inc(x1_sq, 1)
            act.wait_ge(x_var, NT + 2)
            f(rstd, ssq, ACT.Sqrt).then_inc(x_std, 1)
            act.wait_ge(rstd2_ready, 1)
            act.wait_ge(x1_sq, NT)
            def rows_out(t):
                m = rows(t)
                full(act, ("H2", t))
                if t >= 2:
                    act.wait_ge(stored_h2[t % 2], 16 * (t // 2))
                f(h2_row[0:m, t % 2, :], slot[1][0:m, :], ACT.Copy).then_inc(h2_ready, 1)
                act.wait_ge(h2_ready, t + 1)
                act.sem_inc(slots.drained[1], 1)
                full(act, ("R", t))
                empty(f(scores[0:m, t, :], slot[4][0:m, 0:E], ACT.Sigmoid), ("R", t))

            for t in range(NT):
                m = rows(t)
                if t >= 2:
                    full(act, ("X2", t - 2))
                f(h2_tok[0:m, t % 2, :], x1[0:m, t, :], ACT.Copy, scale=rstd[0:m, t:t + 1]).then_inc(xn2_ready, 1)
                if t:
                    rows_out(t - 1)
            rows_out(NT - 1)
            slots.wait_empty(act, ("R", 8))
            slots.wait_empty(act, ("R", 7))
            act.sem_inc(scores_ready, 1)
            for t in range(NT):
                m = rows(t)
                full(act, ("GS", t))
                if t >= 2:
                    act.wait_ge(sh_h, t - 1)
                alink(f(sh_g[0:m, t % 2, :], slot[2 + t % 2][0:m, 0:FE], ACT.Silu))
                f(sh_u[t % 2][0:m, :], slot[2 + t % 2][0:m, FE:2 * FE], ACT.Copy).then_inc(sh_gu_out, 1)
                act.wait_ge(sh_gu_out, t + 1)
                act.sem_inc(slots.drained[2 + t % 2], 1)
                full(act, ("HS", t))
                if t:
                    full(act, ("YS2", t - 1))
                empty(f(hTs[:, :, 0:m], slot[4].rearrange("p (k c) -> p k c", k=4)[:, 0:2, 0:m], ACT.Copy), ("HS", t))
                full(act, ("YS2", t))
                if t >= 2:
                    act.wait_ge(stored_ys[t % 2], 16 * (t // 2))
                ins = f(y_buf[0:m, t % 2, :], slot[t % 2][0:m, :], ACT.Copy)
                ins.then_inc(ys2_ready, 1)
                act.wait_ge(ys2_ready, t + 1)
                act.sem_inc(slots.drained[t % 2], 1)
            act.sem_inc(xt_copied, 1)
            act.sem_inc(y_act, 1)
            act.wait_ge(table_ready, 4)
            n_pairs = act.value_load(n_pairs_t[0:1, 0:1], min_val=1, max_val=MAXPAIR)

            def rows_turned(b, par):
                act.wait_ge(turned, b + 3)
                act.wait_ge(gu_done, b + 1)
                f(xTs[:, par].rearrange("p k c -> p (k c)"), slot[0], ACT.Copy).then_inc(xt_copied, 1)

            def gate(b, par):
                act.wait_ge(gu_done, b + 3)
                act.wait_ge(h_done, b + 1)
                f(e_g[:, par, :], slot[2 + par][:, 0:FE], ACT.Silu).then_inc(g_done, 1)

            rows_turned(0, 0)
            gate(0, 0)
            rows_turned(1, 1)
            act.wait_ge(shared_stored, 1)
            with act.Fori(0, n_pairs) as j:
                for par in range(2):
                    b = j * 2 + par
                    gate(b + 1, 1 - par)
                    rows_turned(b + 2, par)
                    act.wait_ge(down_done, b + 3)
                    act.wait_ge(scatter_done, b + 1)
                    act.wait_ge(idx_done, b + 1)
                    f(y_buf[:, par, 0:512], slot[1][:, 0:512], ACT.Copy, scale=w_all[:, bass.ds(b, 1)]).then_inc(y_act, 1)
            act.wait_ge(weights_in, E)
            for q in range(3):
                for smp in range(2):
                    full(act, ("FR", q, smp))
                    m = NS if smp else P
                    empty(f(fin_rows[0:m, 2 * q + smp, :], slot[smp][0:m, :], ACT.Copy), ("FR", q, smp))
            slots.wait_empty(act, ("FR", 2, 1))
            slots.wait_empty(act, ("FR", 2, 0))
            act.sem_inc(rows_ready, 1)
            for t in range(NT + 1):
                if t < NT:
                    m = rows(t)
                    act.wait_ge(x2_ready, t + 1)
                    if t:
                        act.wait_ge(x2_sq, t)
                    f(sq_junk2[0:m, :], x1[0:m, t, :], ACT.Square, accum_out=ssq[0:m, t:t + 1]).then_inc(x2_sq, 1)
                if t:
                    m = rows(t - 1)
                    act.wait_ge(x_var, NT + 2 + t)
                    f(rstd[0:m, t - 1:t], ssq[0:m, t - 1:t], ACT.Sqrt).then_inc(x_std, 1)

        @block.gpsimd
        def _(pool):
            plink(pool.memset(ident, 0.0))
            pool.affine_select(out=ident, in_=ident, compare_op=ALU.not_equal, fill=1.0, base=0, pattern=[[-1, P]], channel_multiplier=1).then_inc(consts, 1)
            pool.iota(iota_row, pattern=[[1, P]], base=0, channel_multiplier=0, allow_small_or_imprecise_dtypes=True).then_inc(consts, 1)
            pool.iota(iota_part, pattern=[[0, 1]], base=0, channel_multiplier=1, allow_small_or_imprecise_dtypes=True).then_inc(consts, 1)
            plink(pool.memset(ones_col, 1.0))
            plink(pool.memset(ones_b, 1.0))
            pool.affine_select(out=tri, in_=ones_b, compare_op=ALU.is_gt, fill=0.0, base=0, pattern=[[1, P]], channel_multiplier=-1).then_inc(consts, 1)
            plink(pool.memset(causal, 0.0))
            pool.affine_select(out=causal, in_=causal, compare_op=ALU.is_ge, fill=NEG, base=0, pattern=[[-1, P]], channel_multiplier=1).then_inc(consts, 1)
            plink(pool.memset(ssq, 1.0))
            plink(pool.memset(rstd, 1.0))
            plink(pool.memset(rstd_y, 1.0))
            pool.memset(att_one, 0.0).then_inc(consts, 1)
            pool.wait_ge(ld["step"], 16)
            pool.wait_ge(consts, 6)
            pool.tensor_copy(pack2[32:48, :].rearrange("g (a n) -> g a n", a=2), step_raw.unsqueeze(2).to_broadcast([GP, 2, NST])).then_inc(consts, 1)
            pool.wait_ge(consts, 7)
            pool.sem_inc(ones_set, 1)
            slots.wait_full(pool, ("ADT", NADA + NADF - 1))
            pool.memset(M[:, :, :], 0.0).then_inc(m_zero, 1)
            slots.wait_full(pool, ("YT", 8))
            pool.memset(qT[:, :, :], 0.0).then_inc(q_zero, 1)
            pool.wait_ge(fg_ready, 1)
            slots.wait_full(pool, "LF")
            plink(pool.memset(sel_seq[:, :, :], 0.0))
            v4 = sel_seq.rearrange("p b (h s) -> p b h s", h=H)
            plink(pool.affine_select(out=v4, in_=v4, compare_op=ALU.not_equal, fill=1.0, base=0, pattern=[[-CH, NSEQ], [-1, H], [0, CH]], channel_multiplier=1))
            plink(pool.memset(sel_row, 0.0))
            plink(pool.memset(head_mask, 1.0))
            v3 = head_mask.rearrange("p (h d) -> p h d", h=H)
            plink(pool.affine_select(out=v3, in_=v3, compare_op=ALU.is_ge, fill=0.0, base=0, pattern=[[-CH, H], [0, DH]], channel_multiplier=1))
            plink(pool.affine_select(out=v3, in_=v3, compare_op=ALU.is_ge, fill=0.0, base=CH - 1, pattern=[[CH, H], [0, DH]], channel_multiplier=-1))
            slots.wait_full(pool, ("O", len(ATT) - 1))
            plink(pool.memset(q_bd[:, :, :, :], 0.0))
            pool.sem_inc(smp_pool, 1)
            pool.wait_ge(ld["wout"], 64)
            for k in range(KD):
                plink(pool.tensor_scalar(w_out[:, k, :], w_out[:, k, :], pack_t[:, 92 + k:93 + k], None, ALU.mult))
            pool.sem_inc(wout_scaled, 1)
            slots.wait_full(pool, ("W", NT - 1, 1))
            plink(pool.memset(scores[NS:P, 8, :], 0.0))
            pool.sem_inc(pad_scores, 1)
            for t in range(NT):
                m = rows(t)
                pool.wait_ge(sh_gu_out, t + 1)
                if t >= 2:
                    slots.wait_full(pool, ("HS", t - 2))
                pool.tensor_tensor(h_row[0:m, t % 2, :], sh_g[0:m, t % 2, :], sh_u[t % 2][0:m, :], ALU.mult).then_inc(sh_h, 1)
            pool.sem_inc(scatter_done, 2)
            pool.wait_ge(table_ready, 4)
            n_pairs = pool.value_load(n_pairs_t[0:1, 0:1], min_val=1, max_val=MAXPAIR)
            pool.wait_ge(rows_stored, 1)

            def gather(b, par):
                pool.wait_ge(idx_done, b + 1)
                pool.wait_ge(turned, b + 1)
                pool.sem_inc(pool_tick, 1)
                pool.indirect_dma_start(x_rows[:, par, :], None, h2_dram, bass.IndirectOffsetOnAxis(ap=g_idx[:, par:par + 1], axis=0)).then_inc(gathered[par], 16)

            gather(0, 0)
            gather(1, 1)
            gather(2, 0)
            gather(3, 1)
            pool.wait_ge(shared_stored, 1)
            with pool.Fori(0, n_pairs) as j:
                for par in range(2):
                    b = j * 2 + par
                    pool.wait_ge(y_act, b + 2)
                    pool.wait_ge(y_dve, b + 2)
                    pool.sem_inc(pool_tick, 1)
                    pool.indirect_dma_start(y_dram, bass.IndirectOffsetOnAxis(ap=s_idx[:, par:par + 1], axis=0), y_buf[:, par, :], None,
                                            compute_op=ALU.add).then_inc(scattered, 16)
                    gather(b + 4, par)
                    pool.wait_ge(scattered, (b + 1) * 16)
                    pool.sem_inc(scatter_done, 1)
            pool.sem_inc(routed_done, 1)
            for t in range(NT):
                m, s_ = rows(t), int(t == 8)
                pool.wait_ge(y_scaled, t + 1)
                pool.tensor_tensor(x1[0:m, t, :], x1[0:m, t, :], fin_rows[0:m, 4 + s_, :], ALU.add).then_inc(y_out_ready, 1)

        @block.sync
        def _(sp):
            dma = sp.dma_start
            vec = lambda a, n: a.rearrange("l (c p) -> (l c) p", p=P) if n else a.rearrange("(c p) -> c p", p=P)
            dma(cond[0:1, :], ap["c_prompt"]).then_inc(ld["cond"], 16)
            dma(cond[1:NM, :], ap["c_sample"]).then_inc(ld["cond"], 16)
            def load_ada(n):
                if n >= 2:
                    slots.wait_full(sp, ("ADA", n - 2))
                src = ap["w_ada"][0] if n < NADA else ap["w_ada_final"]
                c = (n if n < NADA else n - NADA) * 512
                dma(ada_w[:, n % 2], src[:, c:c + 512].rearrange("(k p) n -> p k n", p=P)).then_inc(ld_ada[n % 2], 16)

            load_ada(0)
            load_ada(1)
            at = 0
            for name, n in (("b_ada", 48), ("b_ada_final", 16), ("g_norm1", 8), ("g_norm2", 8), ("g_final", 8), ("b_glu", 4), ("g_ssm_out", 4), ("g_attn_out", 4)):
                dma(pack[at:at + n, :], vec(ap[name], name not in ("b_ada_final", "g_final"))).then_inc(ld["pack"], 16)
                at += n
            dma(pack2[0:16, :], ap["ssm_lambda_re"].rearrange("l (g a) n -> (l g) (a n)", a=2)).then_inc(ld["pack"], 16)
            dma(pack2[16:32, :], ap["ssm_lambda_im"].rearrange("l (g a) n -> (l g) (a n)", a=2)).then_inc(ld["pack"], 16)
            dma(step_raw, ap["ssm_log_step"].rearrange("l (g a) -> (l g) a", a=2)).then_inc(ld["step"], 16)
            dma(d_raw, ap["ssm_d"][0]).then_inc(ld["pack"], 16)
            for i, n in enumerate(("state_ssm_re", "state_ssm_im")):
                dma(h0_raw[:, i, :], ap[n].rearrange("l b (g a) n -> (l b g) (a n)", a=2)).then_inc(ld["pack"], 16)
            for i, n in enumerate(("ssm_c_re", "ssm_c_im")):
                for hh in range(2):
                    for g_ in range(8):
                        src = ap[n][0].rearrange("(g a) i n -> g i a n", a=2)[8 * hh + g_]
                        dma(c_raw[g_ * GI:(g_ + 1) * GI, 2 * i + hh, :].rearrange("i (a n) -> i a n", a=2), src).then_inc(ld["pack"], 16)
            for i, n in enumerate(("ssm_b_re", "ssm_b_im")):
                dma(b_raw[:, i], ap[n][0].rearrange("(g a) n i -> (a n) g i", a=2)).then_inc(ld["bc"], 16)
            dma(b_fg, ap["b_fgate"].rearrange("l h -> h l")).then_inc(ld["fgate"], 16)
            for t in range(2):
                dma(x_buf[:, t, :], ap["x_prompt"][0].rearrange("(c t) d -> t c d", t=CH)[t]).then_inc(ld_x[t], 16)
            for n in range(2, NADA + NADF):
                load_ada(n)
                if n == 4:
                    dma(w_u, ap["w_in"][0][:, 0:DA].rearrange("(k p) n -> p k n", p=P)).then_inc(ld["wu"], 16)
            sp.wait_ge(k_ready, 1)
            sp.wait_ge(m_zero, 1)
            for c in range(CH):
                dma(M[c * GI:(c + 1) * GI, :, c * GI:P], Ksb[:, :, 0:(CH - c) * GI]).then_inc(toeplitz, 16)
            for t in range(2, NT):
                slots.wait_full(sp, ("X", t - 2))
                src = ap["x_prompt"][0].rearrange("(c t) d -> t c d", t=CH)[t] if t < 8 else ap["x_sample"].rearrange("b s d -> (b s) d")
                dma(x_buf[0:rows(t), t % 2, :], src).then_inc(ld_x[t % 2], 16)
            slots.wait_full(sp, ("X", 7))
            slots.wait_full(sp, ("X", 8))
            dma(w_glu, ap["w_glu"][0].rearrange("(k p) n -> p k n", p=P)).then_inc(ld["wglu"], 16)
            slots.wait_empty(sp, ("U", 8))
            slots.wait_full(sp, ("K", 7))
            slots.wait_full(sp, ("BS", 7))
            for s_ in range(CH):
                dma(u8[:, :, s_, :], u_s[s_:NS:CH, :].rearrange("b (g i) -> b g i", g=G)).then_inc(moved, 16)
            slots.wait_empty(sp, "FIN")
            for ri, (n1, n2) in enumerate((("ssm_re_prompt", "ssm_re_sample"), ("ssm_im_prompt", "ssm_im_sample"))):
                store(sp, out[n1][0, 0].rearrange("(g a) n -> g (a n)", a=2), fin_out[0:GP, 0, ri * P:(ri + 1) * P])
                store(sp, out[n2][0].rearrange("b (g a) n -> (b g) (a n)", a=2), fin_out[:, 1, ri * P:(ri + 1) * P])
            slots.wait_empty(sp, ("Y", 7, 1))
            slots.wait_empty(sp, ("Y", 6, 1))
            for s_ in range(CH):
                dma(y_s[s_:NS:CH, :], y8[:, s_, :, :].rearrange("b g i -> b (g i)")).then_inc(moved, 16)
            sp.wait_ge(stored, n_stored[0])
            sp.wait_ge(moved, 2 * CH * 16)
            slots.wait_full(sp, ("Y", 7, 1))
            slots.wait_empty(sp, ("S", 15))
            sp.wait_ge(fin_ready, 1)
            dma(w_q, ap["w_in"][0][:, DA:].rearrange("(k p) n -> p k n", p=P)).then_inc(ld["wq"], 16)
            for t in range(NT):
                slots.wait_empty(sp, ("KT", t))
                dst = out["k_prompt"][0, 0].rearrange("t h d -> t (h d)")[t * P:(t + 1) * P] if t < 8 else out["k_sample"][0].rearrange("b s h d -> (b s) (h d)")
                store(sp, dst, k_tok[0:rows(t), t % 2, :], stored_k[t % 2])
                slots.wait_empty(sp, ("V", t))
                dst = out["v_prompt"][0, 0].rearrange("t h d -> t (h d)")[t * P:(t + 1) * P] if t < 8 else out["v_sample"][0].rearrange("b s h d -> (b s) (h d)")
                store(sp, dst, v[0:rows(t), t, :])
            slots.wait_empty(sp, "LF")
            store(sp, out["logf_prompt"][0, 0].rearrange("(t p) h -> p t h", p=P), lf_tok[:, 0:CH * H].rearrange("p (t h) -> p t h", t=CH))
            store(sp, out["logf_sample"][0].rearrange("b s h -> (b s) h"), lf_tok[0:NS, CH * H:NT * H])
            dma(pages_t, ap["page_table"].rearrange("b j -> (b j)").unsqueeze(0)).then_inc(ld_pt, 16)
            sp.wait_ge(fg_ready, 1)
            slots.wait_full(sp, "LF")
            sp.wait_ge(ld_pt, 16)
            for b in range(NSEQ):
                for j in range(PAGES):
                    i = b * PAGES + j
                    pg = sp.value_load(pages_t[0:1, i:i + 1], min_val=0, max_val=N_PHYS - 1)
                    dma(lf_pages[:, j, b * H:(b + 1) * H], ap["cache_logf"][0, bass.ds(pg, 1)].rearrange("a p h -> (a p) h")).then_inc(ld_lfp, 16) 
                dma(lf_s[b * H:(b + 1) * H, PAST:PAST + CH], lf[:, SEQ + b * CH:SEQ + (b + 1) * CH]).then_inc(lf_moved, 16)
            def load_pages(b, dst, src, done):
                for j in range(PAGES):
                    i = b * PAGES + j
                    pg = sp.value_load(pages_t[0:1, i:i + 1], min_val=0, max_val=N_PHYS - 1)
                    dma(dst[:, b % 2, j, :], ap[src][0, bass.ds(pg, 1)].rearrange("a p h d -> (a p) (h d)")).then_inc(done[b % 2], 16)

            for b in range(NSEQ):
                if b >= 2:
                    slots.wait_full(sp, ("SK", b - 2, 3))
                load_pages(b, kpg, "cache_k", ld_page)
                if b >= 2:
                    slots.wait_full(sp, ("SO", b - 2))
                if b == 0:
                    sp.wait_ge(stored_k[0], 16 * 5)
                    sp.wait_ge(stored_k[1], 16 * 4)
                dma(v_new[:, b % 2, :], v[b * CH:(b + 1) * CH, 8, :]).then_inc(ld_vnew[b % 2], 16)
                load_pages(b, vpg, "cache_v", ld_vpage)
                if 3 <= b < 7:
                    if b == 3:
                        sp.wait_ge(smp_q, 1)
                    k0 = 2 * (b - 3)
                    dma(w_out[:, k0:k0 + 2, :], ap["w_out"][0].rearrange("(k p) n -> p k n", p=P)[:, k0:k0 + 2, :]).then_inc(ld["wout"], 16)
            slots.wait_full(sp, ("SL", 7))
            slots.wait_full(sp, ("SO", 7))
            sp.wait_ge(stored, n_stored[0])
            dma(w_router, ap["w_router"][0].rearrange("(k p) n -> p k n", p=P)).then_inc(ld["router"], 16)
            slots.wait_full(sp, "SR")
            dma(x1[:, 0:8, :], ap["x_prompt"][0].rearrange("(c t) d -> c t d", t=CH)).then_inc(ld_res, 16)
            dma(x1[0:NS, 8, :], ap["x_sample"].rearrange("b s d -> (b s) d")).then_inc(ld_res, 16)
            slots.wait_full(sp, ("OT", 8))
            slots.wait_full(sp, ("OT", 7))
            dma(sh_gu[:, :, 0:FE], ap["w_sh_gate"][0].rearrange("(k p) n -> p k n", p=P)).then_inc(ld_shared, 16)
            dma(sh_gu[:, :, FE:], ap["w_sh_up"][0].rearrange("(k p) n -> p k n", p=P)).then_inc(ld_shared, 16)
            dma(sh_d, ap["w_sh_down"][0].rearrange("(k p) n -> p k n", p=P)).then_inc(ld_shared, 16)
            slots.wait_full(sp, ("W", NT - 1, 1))
            dma(r_bias, ap["router_bias"].to_broadcast([P, E])).then_inc(ld_rb, 16)
            for t in range(NT):
                sp.wait_ge(h2_ready, t + 1)
                store(sp, h2_dram[t * P:t * P + rows(t), :], h2_row[0:rows(t), t % 2, :], stored_h2[t % 2])
            sp.wait_ge(stored_h2[0], 80)
            sp.wait_ge(stored_h2[1], 64)
            sp.sem_inc(rows_stored, 1)
            for t in range(NT - 1):
                sp.wait_ge(ys2_ready, t + 1)
                store(sp, y_dram[t * P:t * P + rows(t), :], y_buf[0:rows(t), t % 2, :], stored_ys[t % 2])
            eg = ap["w_exp_gate"][0].rearrange("e (k p) n -> e p k n", p=P)
            eu = ap["w_exp_up"][0].rearrange("e (k p) n -> e p k n", p=P)
            ed = ap["w_exp_down"][0].rearrange("e (k p) (c n) -> e p k c n", p=P, c=2)

            def load_expert(n, q):
                release = sp.value_load(release_i[0:1, bass.ds(n, 1)], min_val=2, max_val=MAXBLK)
                e = sp.value_load(order_i[0:1, bass.ds(n, 1)], min_val=0, max_val=E - 1)
                dst = ring[:, RING - 1 - q]
                sp.wait_ge(down_done, release)
                dma(dst[:, 0:KD, 0:FE], eg[bass.ds(e, 1)].rearrange("a p k n -> (a p) k n")).then_inc(ld_ring[q], 16)
                dma(dst[:, 0:KD, FE:], eu[bass.ds(e, 1)].rearrange("a p k n -> (a p) k n")).then_inc(ld_ring[q], 16)
                dma(dst[:, KD:, :].rearrange("p (k c) n -> p k c n", k=2), ed[bass.ds(e, 1)].rearrange("a p k c n -> (a p) k c n")).then_inc(ld_ring[q], 16)

            sp.wait_ge(table_ready, 4)
            slots.wait_full(sp, ("W", NT - 1, 1))
            load_expert(0, 0)
            t = NT - 1
            sp.wait_ge(ys2_ready, NT)
            store(sp, y_dram[t * P:t * P + rows(t), :], y_buf[0:rows(t), t % 2, :], stored_ys[t % 2])
            dma(y_dram[T:, :], y_zero).then_inc(stored_ys[1], 16)
            sp.wait_ge(stored_ys[0], 80)
            sp.wait_ge(stored_ys[1], 80)
            sp.sem_inc(shared_stored, 1)
            sp.wait_ge(ld_ring[0], 48)
            sp.sem_inc(weights_in, 1)
            with sp.Fori(0, E // RING - 1) as j:
                for i in range(RING):
                    q = (i + 1) % RING
                    load_expert(j * RING + (i + 1), q)
                    sp.wait_ge(ld_ring[q], (j + 1) * 48 if q else (j + 2) * 48)
                    sp.sem_inc(weights_in, 1)
            for q in range(1, RING):
                load_expert(E - RING + q, q)
                sp.wait_ge(ld_ring[q], 48 * (E // RING))
                sp.sem_inc(weights_in, 1)
            sp.wait_ge(routed_done, 1)
            for t in range(NT):
                dma(y_rows[0:rows(t), t, :], y_dram[t * P:t * P + rows(t), :]).then_inc(ld_y[t], 16)
            for t in range(NT):
                sp.wait_ge(y_out_ready, t + 1)
                dst = out["y_prompt"][0].rearrange("(c t) d -> t c d", t=CH)[t] if t < 8 else out["y_sample"].rearrange("b s d -> (b s) d")
                store(sp, dst, x1[0:rows(t), t, :])
            sp.wait_ge(stored, n_stored[0])
            sp.wait_ge(stored_k[0], 80)
            sp.wait_ge(stored_k[1], 64)


_INS = ['x_prompt', 'x_sample', 'c_prompt', 'c_sample', 'cache_k', 'cache_v', 'cache_logf', 'state_ssm_re', 'state_ssm_im', 'page_table',
        'w_ada', 'b_ada', 'g_norm1', 'w_in', 'b_fgate', 'ssm_lambda_re', 'ssm_lambda_im', 'ssm_log_step', 'ssm_b_re', 'ssm_b_im',
        'ssm_c_re', 'ssm_c_im', 'ssm_d', 'w_glu', 'b_glu', 'g_ssm_out', 'g_attn_out', 'w_out', 'g_norm2', 'w_router', 'router_bias',
        'w_exp_gate', 'w_exp_up', 'w_exp_down', 'w_sh_gate', 'w_sh_up', 'w_sh_down', 'g_final', 'w_ada_final', 'b_ada_final']
_OUTS = [('y_prompt', (1, SEQ, D)), ('y_sample', (NSEQ, CH, D)),
         ('k_prompt', (1, 1, SEQ, H, DH)), ('v_prompt', (1, 1, SEQ, H, DH)), ('logf_prompt', (1, 1, SEQ, H)),
         ('ssm_re_prompt', (1, 1, G, NST)), ('ssm_im_prompt', (1, 1, G, NST)),
         ('k_sample', (1, NSEQ, CH, H, DH)), ('v_sample', (1, NSEQ, CH, H, DH)), ('logf_sample', (1, NSEQ, CH, H)),
         ('ssm_re_sample', (1, NSEQ, G, NST)), ('ssm_im_sample', (1, NSEQ, G, NST))]


def kernel(**inputs):
    import numpy as _np
    import concourse.bacc as _bacc
    from concourse import mybir as _mybir
    from concourse.bass_utils import run_bass_kernel_spmd as _run

    nc = _bacc.Bacc("TRN2", target_bir_lowering=False, num_devices=1)
    arrays, ap, out = {}, {}, {}
    for name in _INS:
        a = _np.ascontiguousarray(inputs[name])
        arrays[f"in_{name}"] = a
        ap[name] = nc.dram_tensor(f"in_{name}", a.shape, _mybir.dt.from_np(a.dtype), kind="ExternalInput").ap()
    for name, shape in _OUTS:
        out[name] = nc.dram_tensor(f"out_{name}", shape, _mybir.dt.float32, kind="ExternalOutput").ap()
    hymba_program(nc, ap, out)
    r = _run(nc, [arrays], core_ids=[0])
    return tuple(r.results[0][f"out_{name}"] for name, _ in _OUTS)
```
